# Optimizing a Trainium2 kernel written in Bass

```python
import jax, jax.numpy as jnp
from jax import lax
import numpy as np

D_MODEL = 1024
BATCH = 1
SEQ = 256
DEPTH = 1
DEC_BATCH = 8
DEC_SEQ = 4
PAST_LEN = 2048
PAGE_SIZE = 128

D_MIX = D_MODEL
D_CONV = D_MIX // 2
D_POOL = D_MIX - D_CONV
CONV_HEADS = 8
CONV_W = 3
POOL_WINDOWS = (2, 4, 8, 16)
N_POOL_GROUPS = len(POOL_WINDOWS)
POOL_GROUP = D_POOL // N_POOL_GROUPS
POOL_BUF = max(POOL_WINDOWS) - 1
D_IN = 3 * D_CONV + D_POOL
N_EXPERTS = 32
TOP_K = 4
D_FF = D_MODEL
SWIGLU_LIMIT = 7.0
SWIGLU_ALPHA = 1.702
EPS = 1e-5

kernel_name = "hymba_conv_pool_moe_step"

def rmsnorm(x, g):
    xf = x.astype(jnp.float32)
    y = xf * lax.rsqrt(jnp.mean(xf * xf, axis=-1, keepdims=True) + EPS)
    return (y * g.astype(jnp.float32)).astype(x.dtype)

def conv_mixer(pc, buf, conv_w):
    b_gate = pc[..., :D_CONV]
    c_gate = pc[..., D_CONV:2 * D_CONV]
    h = pc[..., 2 * D_CONV:]
    u = c_gate * h
    s = u.shape[1]
    up = jnp.concatenate([buf.astype(u.dtype), u], axis=1)
    y = up[:, 0:s] * conv_w[0]
    for k in range(1, CONV_W):
        y = y + up[:, k:k + s] * conv_w[k]
    return b_gate * y, up[:, -(CONV_W - 1):]

def pool_mixer(v, buf, start_pos, pool_w, pool_scale):
    s = v.shape[1]
    vp = jnp.concatenate([buf.astype(v.dtype), v], axis=1)
    vf = vp.astype(jnp.float32)
    cs = jnp.concatenate([jnp.zeros_like(vf[:, :1]), jnp.cumsum(vf, axis=1)], axis=1)
    hi = cs[:, POOL_BUF + 1:POOL_BUF + 1 + s]
    pos = (start_pos + jnp.arange(s, dtype=jnp.int32)).astype(jnp.float32)
    vfx = v.astype(jnp.float32)
    outs = []
    for g, w in enumerate(POOL_WINDOWS):
        sl = slice(g * POOL_GROUP, (g + 1) * POOL_GROUP)
        lo = cs[:, POOL_BUF + 1 - w:POOL_BUF + 1 - w + s, sl]
        cnt = jnp.minimum(jnp.float32(w), pos + 1.0)[None, :, None]
        outs.append((hi[..., sl] - lo) / cnt - vfx[..., sl])
    p = jnp.stack(outs, axis=2).astype(v.dtype)
    z = jnp.einsum('bsgc,gcd->bsgd', p, pool_w).reshape(v.shape)
    return z * pool_scale, vp[:, -POOL_BUF:]

def moe(x, router_w, router_b, w1, b1, w2, b2):
    shp = x.shape
    xt = x.reshape(-1, shp[-1])
    logits = xt.astype(jnp.float32) @ router_w.astype(jnp.float32) + router_b.astype(jnp.float32)
    vals, idx = lax.top_k(logits, TOP_K)
    gates = jax.nn.softmax(vals, axis=-1)
    combine = jnp.sum(jax.nn.one_hot(idx, N_EXPERTS, dtype=jnp.float32) * gates[..., None], axis=1)
    combine = combine.astype(x.dtype)
    acc = jnp.zeros_like(xt)
    for e in range(N_EXPERTS):
        gu = xt @ w1[e] + b1[e]
        gate = jnp.minimum(gu[:, :D_FF], SWIGLU_LIMIT)
        lin = jnp.clip(gu[:, D_FF:], -SWIGLU_LIMIT, SWIGLU_LIMIT)
        glu = gate * jax.nn.sigmoid(SWIGLU_ALPHA * gate)
        out = (glu * (lin + 1.0)) @ w2[e] + b2[e]
        acc = acc + combine[:, e:e + 1] * out
    return acc.reshape(shp)

def layer(x, conv_buf, pool_buf, start_pos, l, norm_mix_g, w_in, conv_w, pool_w, pool_scale,
          w_out, norm_ffn_g, router_w, router_b, exp_w1, exp_b1, exp_w2, exp_b2):
    xn = rmsnorm(x, norm_mix_g[l])
    proj = jnp.einsum('bsd,de->bse', xn, w_in[l])
    zc, new_conv = conv_mixer(proj[..., :3 * D_CONV], conv_buf, conv_w[l])
    zp, new_pool = pool_mixer(proj[..., 3 * D_CONV:], pool_buf, start_pos, pool_w[l], pool_scale[l])
    z = jnp.concatenate([zc, zp], axis=-1)
    x = x + jnp.einsum('bse,ed->bsd', z, w_out[l])
    x = x + moe(rmsnorm(x, norm_ffn_g[l]), router_w[l], router_b[l],
                exp_w1[l], exp_b1[l], exp_w2[l], exp_b2[l])
    return x, new_conv, new_pool

def setup_inputs(seed: int = 0) -> dict:
    key = jax.random.key(seed)
    ks = jax.random.split(key, 20)
    f = jnp.float32
    n = lambda k, s, sc: jax.random.normal(k, s, f) * sc
    return {
        "x_prompt": n(ks[0], (BATCH, SEQ, D_MODEL), 1.0),
        "x_sample": n(ks[1], (DEC_BATCH, DEC_SEQ, D_MODEL), 1.0),
        "state_conv": n(ks[2], (DEPTH, DEC_BATCH, CONV_W - 1, D_CONV), 1.0),
        "state_pool": n(ks[3], (DEPTH, DEC_BATCH, POOL_BUF, D_POOL), 1.0),
        "norm_mix_g": 1.0 + n(ks[4], (DEPTH, D_MODEL), 0.01),
        "w_in": n(ks[5], (DEPTH, D_MODEL, D_IN), D_MODEL ** -0.5),
        "conv_w": n(ks[6], (DEPTH, CONV_W, D_CONV), CONV_W ** -0.5),
        "pool_w": n(ks[7], (DEPTH, N_POOL_GROUPS, POOL_GROUP, POOL_GROUP), POOL_GROUP ** -0.5),
        "pool_scale": 1.0 + n(ks[8], (DEPTH, D_POOL), 0.1),
        "w_out": n(ks[9], (DEPTH, D_MIX, D_MODEL), D_MIX ** -0.5),
        "norm_ffn_g": 1.0 + n(ks[10], (DEPTH, D_MODEL), 0.01),
        "router_w": n(ks[11], (DEPTH, D_MODEL, N_EXPERTS), D_MODEL ** -0.5),
        "router_b": n(ks[12], (DEPTH, N_EXPERTS), 0.01),
        "exp_w1": n(ks[13], (DEPTH, N_EXPERTS, D_MODEL, 2 * D_FF), D_MODEL ** -0.5),
        "exp_b1": n(ks[14], (DEPTH, N_EXPERTS, 2 * D_FF), 0.01),
        "exp_w2": n(ks[15], (DEPTH, N_EXPERTS, D_FF, D_MODEL), D_FF ** -0.5),
        "exp_b2": n(ks[16], (DEPTH, N_EXPERTS, D_MODEL), 0.01),
        "final_norm_g": 1.0 + n(ks[17], (D_MODEL,), 0.01),
    }

def reference(x_prompt, x_sample, state_conv, state_pool, norm_mix_g, w_in, conv_w, pool_w,
              pool_scale, w_out, norm_ffn_g, router_w, router_b, exp_w1, exp_b1, exp_w2,
              exp_b2, final_norm_g):
    params = (norm_mix_g, w_in, conv_w, pool_w, pool_scale, w_out, norm_ffn_g,
              router_w, router_b, exp_w1, exp_b1, exp_w2, exp_b2)
    hp = x_prompt
    hs = x_sample
    cp_list, pp_list, cs_list, ps_list = [], [], [], []
    for l in range(DEPTH):
        zero_conv = jnp.zeros((x_prompt.shape[0], CONV_W - 1, D_CONV), x_prompt.dtype)
        zero_pool = jnp.zeros((x_prompt.shape[0], POOL_BUF, D_POOL), x_prompt.dtype)
        hp, ncp, npp = layer(hp, zero_conv, zero_pool, 0, l, *params)
        hs, ncs, nps = layer(hs, state_conv[l], state_pool[l], PAST_LEN, l, *params)
        cp_list.append(ncp); pp_list.append(npp)
        cs_list.append(ncs); ps_list.append(nps)
    y_prompt = rmsnorm(hp, final_norm_g)
    y_sample = rmsnorm(hs, final_norm_g)
    new_conv_prompt = jnp.stack(cp_list, axis=0)
    new_pool_prompt = jnp.stack(pp_list, axis=0)
    new_conv_sample = jnp.stack(cs_list, axis=0)
    new_pool_sample = jnp.stack(ps_list, axis=0)
    return (y_prompt, y_sample, new_conv_prompt, new_pool_prompt, new_conv_sample, new_pool_sample)


_drawn_inputs = setup_inputs


def setup_inputs(seed=0):
    import zlib

    import numpy as np

    out = dict(_drawn_inputs(seed))
    spreads = {}
    factors = {'router_b': 2.938, 'exp_b1': 8.0, 'exp_b2': 8.0, 'final_norm_g': 5.725}
    for name, (base, spread) in spreads.items():
        noise = np.random.default_rng([zlib.crc32(name.encode()), seed]).standard_normal(out[name].shape)
        drawn = base * np.exp(spread * noise) if base else spread * noise
        out[name] = __import__('jax').numpy.asarray(drawn.astype(out[name].dtype))
    for name, factor in factors.items():
        out[name] = (out[name] * factor).astype(out[name].dtype)
    return out
```

```python
from contextlib import ExitStack

import concourse.bass as bass
from concourse import mybir

F32 = mybir.dt.float32
I32 = mybir.dt.int32
U32 = mybir.dt.uint32
ALU = mybir.AluOpType
ACT = mybir.ActivationFunctionType
AX = mybir.AxisListType

P = 128
BANK = 512
SWIGLU_LIMIT = 7.0
SWIGLU_ALPHA = 1.702
EPS = 1e-5
TOP_K = 4
WINDOWS = (2, 4, 8, 16)
SLOTS = 64


class Counter:

    def __init__(self, sem):
        self.sem, self.base, self.n = sem, 0, 0

    def inc(self, instruction, by=1):
        instruction.then_inc(self.sem, by)
        self.n += by

    def now(self):
        return self.base + self.n


def hybrid_moe_layer(nc, x_prompt, x_sample, state_conv, state_pool, norm_mix_g, w_in, conv_w,
                     pool_w, pool_scale, w_out, norm_ffn_g, router_w, router_b, exp_w1, exp_b1,
                     exp_w2, exp_b2, final_norm_g, y_prompt, y_sample, new_conv_prompt,
                     new_pool_prompt, new_conv_sample, new_pool_sample):
    _, NP, D = x_prompt.shape
    NB, NT, _ = x_sample.shape
    NS = NB * NT
    T = NP + NS
    DC, DPL = state_conv.shape[3], state_pool.shape[3]
    CB, PB = state_conv.shape[2], state_pool.shape[2]
    E = router_w.shape[2]
    F = exp_w2.shape[2]
    KD = D // P
    KC = DC // P
    NTILE = (T + P - 1) // P
    rows = [min(P, T - P * t) for t in range(NTILE)]
    NG = len(WINDOWS)
    PAIRS = E // 2
    ROUNDS = (T + SLOTS - 1) // SLOTS
    W1N = 2 * F // BANK
    YN = D // BANK
    assert NP == 2 * P and NS == 32 and D == F and DC == DPL and KC == NG and D % BANK == 0

    CL = CB + NP + NB * (CB + NT)
    PL = PB + NP + NB * (PB + NT)
    CS, PS = CB + NP, PB + NP
    CY = CL - CB

    ctx = ExitStack()
    with ctx:
        def sb(name, shape, dt=F32):
            return ctx.enter_context(nc.sbuf_tensor(name, shape, dt))

        def sem(name):
            return ctx.enter_context(nc.semaphore(name))

        w1_ring = sb("w1_ring", [P, 4, 2, 2 * F])
        w2_ring = sb("w2_ring", [P, 4, 2, 2, D])
        x_acc = sb("x_acc", [P, NTILE, D])
        x_norm = sb("x_norm", [P, NTILE, D])
        hidden = sb("hidden", [P, 3, 2, BANK])
        routed = sb("routed", [P, 3, 1024])
        b1_rows = sb("b1_rows", [E, 2 * F])
        b2_rows = sb("b2_rows", [E, D])
        g_ffn = sb("g_ffn", [P, D])
        back = sb("back", [P, T])
        place = sb("place", [P, NTILE, 2, SLOTS])
        gated = sb("gated", [P, NTILE, 2, SLOTS])
        pick_b1 = sb("pick_b1", [E, 2, SLOTS])
        ident = sb("ident", [P, P])
        before = sb("before", [P, P])
        ones = sb("ones", [P, P])
        slot_id = sb("slot_id", [P, SLOTS])
        expert_id = sb("expert_id", [P, E])
        vec_rows = sb("vec_rows", [4 * KD, P])
        vecs = sb("vecs", [P, 4 * KD])
        router_f = sb("router_f", [P, KD, E])
        router_g = sb("router_g", [P, KD, E])
        bias_e = sb("bias_e", [P, E])
        pool_f = sb("pool_f", [P, NG, P])
        fix = sb("fix", [P, NG, 16])
        ramp = sb("ramp", [P, 16])
        sumsq = sb("sumsq", [P, 3, NTILE])
        rms = sb("rms", [P, 3, NTILE])
        half = sb("half", [P, NTILE])
        logits = sb("logits", [P, NTILE, E])
        top8 = sb("top8", [P, NTILE, 8])
        top_at = sb("top_at", [P, NTILE, 8], U32)
        top_f = sb("top_f", [P, NTILE, 8])
        mask = sb("mask", [P, NTILE, E])
        shifted = sb("shifted", [P, NTILE, E])
        combine = sb("combine", [P, NTILE, E + 2])
        rank = sb("rank", [P, NTILE, E + 2])
        denom = sb("denom", [P, NTILE])
        combine_t = sb("combine_t", [E, T])
        most = sb("most", [P, 1])
        most_i = sb("most_i", [P, 1], I32)
        psum = ctx.enter_context(nc.psum_tensor("psum", [P, 8, BANK], F32))

        w_in_sb = w1_ring[:].rearrange("p s e n -> p s (e n)").rearrange("p s (k n) -> p s k n", k=KD)
        w2_flat = w2_ring[:].rearrange("p s e k n -> p (s e k n)")
        w_out_sb = w2_flat[:, 0:KD * D].rearrange("p (k n) -> p k n", k=KD)
        at = KD * D

        def scratch(blocks, length):
            nonlocal at
            v = w2_flat[:, at:at + blocks * length].rearrange("p (k n) -> p k n", k=blocks)
            at += blocks * length
            return v

        u_pad = scratch(KC, CL)
        v_pad = scratch(NG, PL)
        sum_a = scratch(NG, PL)
        sum_b = scratch(NG, PL)
        conv_y = scratch(KC, CL)
        assert at <= 4 * 4 * D
        flat_h = hidden[:].rearrange("p a b n -> p (a b n)")
        x_t = flat_h[:, 0:KD * T].rearrange("p (k n) -> p k n", k=KD)
        flat_r = routed[:].rearrange("p a n -> p (a n)")
        match = flat_h[:, KD * T:KD * T + NTILE * E * TOP_K].rearrange("p (t e k) -> p t e k", t=NTILE, k=TOP_K)
        z_t = flat_r[:, 0:KD * T].rearrange("p (k n) -> p k n", k=KD)
        flat_n = x_norm[:].rearrange("p a n -> p (a n)")
        c_gate = flat_n[:, 0:KC * T].rearrange("p (k n) -> p k n", k=KC)
        p_t = c_gate
        conv_rows = flat_r[0:NB * CB, KD * T:KD * T + DC]
        pool_rows = w2_flat[0:NB * PB, KD * D + KC * CL + 2 * NG * PL:KD * D + KC * CL + 2 * NG * PL + DPL]
        cache_rows = w2_flat[:, KD * D + KC * CL + NG * PL:KD * D + KC * CL + NG * PL + 4 * DC].rearrange(
            "p (k n) -> p k n", k=4)
        after_rows = KD * D + KC * CL + NG * PL + 4 * DC
        u_last = w2_flat[:, after_rows:after_rows + KC * NB * CB].rearrange("p (k n) -> p k n", k=KC)
        after_rows += KC * NB * CB
        v_last = w2_flat[:, after_rows:after_rows + NG * NS].rearrange("p (k n) -> p k n", k=NG)
        assert after_rows + NG * NS <= KD * D + KC * CL + 3 * NG * PL
        g_final = routed[:, 2, :]
        gathered_t = routed[:, 0, :].rearrange("p (k e s) -> p k e s", k=KD, e=2)
        h_t = routed[:, 1, :].rearrange("p (k e s) -> p k e s", k=KD, e=2)
        y_slots = routed[:, 2, :].rearrange("p (n c) -> p n c", n=YN)

        G_MIX, CONV_W, SCALE, G_FFN = 0, KD, KD + 3 * KC, 2 * KD + 2 * KC
        assert G_FFN == 3 * KD

        x_landed = [sem(f"x_landed{t}") for t in range(NTILE)]
        w_in_landed = [sem(f"w_in_landed{j}") for j in range(4)]
        w_out_landed = sem("w_out_landed")
        vecs_landed = sem("vecs_landed")
        states_landed = sem("states_landed")
        consts_landed = sem("consts_landed")
        w1_landed = [sem(f"w1_landed{s}") for s in range(4)]
        w2_landed = [sem(f"w2_landed{s}") for s in range(4)]
        g_final_landed = sem("g_final_landed")
        stored = sem("stored")
        dve_step = sem("dve_step")
        pool_step = sem("pool_step")
        consts_made = sem("consts_made")
        presets_made = sem("presets_made")
        v_ready = sem("v_ready")
        last_ready = sem("last_ready")
        cache_read = sem("cache_read")
        cache_stored = sem("cache_stored")
        squares = sem("squares")
        rms_ready = sem("rms_ready")
        scaled = sem("scaled")
        front_t = sem("front_t")
        front_t_read = sem("front_t_read")
        x_t_ready = sem("x_t_ready")
        x_t_dve = sem("x_t_dve")
        x_t_act = sem("x_t_act")
        proj_read = sem("proj_read")
        u_ready = sem("u_ready")
        pooled = sem("pooled")
        z_pool_ready = sem("z_pool_ready")
        z_ready = sem("z_ready")
        mixed = sem("mixed")
        residual = sem("residual")
        logits_ready = sem("logits_ready")
        cache_ready = sem("cache_ready")
        shifted_ready = sem("shifted_ready")
        exp_ready = sem("exp_ready")
        mask_ready = sem("mask_ready")
        ranks_ready = sem("ranks_ready")
        combine_ready = sem("combine_ready")
        combine_t_ready = sem("combine_t_ready")
        combine_t_read = sem("combine_t_read")
        b2_ready = sem("b2_ready")
        b2_added = sem("b2_added")
        counts_ready = sem("counts_ready")
        w1_used = sem("w1_used")
        w2_used = sem("w2_used")
        slots_ready = sem("slots_ready")
        gathered = sem("gathered")
        gathered_read = sem("gathered_read")
        back_ready = sem("back_ready")
        back_read = sem("back_read")
        bias_added = sem("bias_added")
        dve_build = sem("dve_build")
        slot_step = sem("slot_step")
        lin_step = sem("lin_step")
        moe_done = sem("moe_done")
        gate_ready = sem("gate_ready")
        sig_ready = sem("sig_ready")
        h_ready = sem("h_ready")
        h_t_ready = sem("h_t_ready")
        h_t_read = sem("h_t_read")
        y_read = sem("y_read")
        spread = sem("spread")
        spread_read = sem("spread_read")
        final_ready = sem("final_ready")

        block = ctx.enter_context(nc.Block())

        def reg(engine, value, top):
            return value if isinstance(value, int) else engine.snap(value, min_val=0, max_val=top)

        def rounds_after_first(engine, run):
            tokens = engine.value_load(most_i[0:1, 0:1], min_val=0, max_val=T)
            with engine.Fori(1, ROUNDS) as r:
                with engine.If(tokens > r * SLOTS):
                    run(r)
                engine.nop()

        @block.sync
        def _(sp):
            nc.sync.dma_start(x_acc[:, 0, :], x_prompt[0][0:P, :]).then_inc(x_landed[0], 16)
            nc.sync.dma_start(x_acc[:, 1, :], x_prompt[0][P:2 * P, :]).then_inc(x_landed[1], 16)
            nc.sync.dma_start(x_acc[0:NS, 2, :], x_sample.rearrange("b t d -> (b t) d")).then_inc(x_landed[2], 16)
            for j, col in enumerate((1, 2, 3, 0)):
                nc.sync.dma_start(w_in_sb[:, j], w_in[0][:, col * DC:(col + 1) * DC].rearrange(
                    "(k p) n -> p k n", p=P)).then_inc(w_in_landed[j], 16)
            nc.sync.dma_start(w_out_sb, w_out[0].rearrange("(k p) n -> p k n", p=P)).then_inc(w_out_landed, 16)

            def load_w1(pair, k, n):
                sp.wait_ge(w1_used, n * KD + k + 1)
                nc.sync.dma_start(w1_ring[:, k % 4], exp_w1[0][bass.ds(pair * 2, 2), k * P:(k + 1) * P, :]
                                  .rearrange("e p n -> p e n")).then_inc(w1_landed[k % 4], 16)

            def load_w2(pair, s, n):
                sp.wait_ge(w2_used, n * 4 + s + 1)
                for e in range(2):
                    nc.sync.dma_start(w2_ring[:, s, e], exp_w2[0][bass.ds(pair * 2 + e, 1), s * 2 * P:(s + 1) * 2 * P, :]
                                      .rearrange("e (k p) n -> p (e k) n", p=P)).then_inc(w2_landed[s], 16)

            def round_of(r):
                with nc.sync.Fori(0, PAIRS) as pair:
                    n = reg(nc.sync, r * PAIRS + pair, ROUNDS * PAIRS)
                    for k in range(KD):
                        load_w1(pair, k, n)
                    for s in range(4):
                        load_w2(pair, s, n)

            round_of(0)
            sp.wait_ge(counts_ready, 1)
            rounds_after_first(nc.sync, round_of)

            for t in range(NTILE):
                sp.wait_ge(final_ready, t + 1)
                dst = y_prompt[0][t * P:(t + 1) * P, :] if t < 2 else y_sample.rearrange("b t d -> (b t) d")
                nc.sync.dma_start(dst, x_norm[0:rows[t], t, :]).then_inc(stored, 16)
            sp.wait_ge(stored, 16 * (NTILE + 1))
            sp.wait_ge(cache_stored, 16 * (3 + NB))

        @block.tensor
        def _(pe):
            mm = nc.tensor.matmul

            pe.wait_ge(consts_made, 1)
            pe.wait_ge(vecs_landed, 16 * 4)
            nc.tensor.transpose(psum[:, 0, 0:4 * KD], vec_rows[:], ident[0:4 * KD, 0:4 * KD]).then_inc(front_t, 1)
            pe.wait_ge(states_landed, 16 * 2)
            for j in range(KC):
                last = nc.tensor.transpose(psum[:, 1, 16 * j:16 * j + NB * CB], conv_rows[:, j * P:(j + 1) * P],
                                           ident[0:NB * CB, 0:NB * CB])
            last.then_inc(front_t, 1)
            for j in range(NG):
                last = nc.tensor.transpose(psum[:, 2, P * j:P * j + NB * PB], pool_rows[:, j * P:(j + 1) * P],
                                           ident[0:NB * PB, 0:NB * PB])
            last.then_inc(front_t, 1)

            pe.wait_ge(scaled, NTILE)
            pe.wait_ge(front_t_read, 3)
            for k in range(KD):
                for t in range(NTILE):
                    last = nc.tensor.transpose(psum[:, k, t * P:t * P + rows[t]],
                                               x_norm[0:rows[t], t, k * P:(k + 1) * P],
                                               ident[0:rows[t], 0:rows[t]])
                last.then_inc(x_t_ready, 1)

            pe.wait_ge(x_t_dve, KD // 2)
            pe.wait_ge(x_t_act, KD // 2)
            for j in range(4):
                pe.wait_ge(w_in_landed[j], 16)
                if j >= 2:
                    pe.wait_ge(proj_read, j - 1)
                for m in range(KC):
                    for k in range(KD):
                        last = mm(psum[:, 4 * (j % 2) + m, 0:T], w_in_sb[:, j, k, m * P:(m + 1) * P],
                                  x_t[:, k, :], start=(k == 0), stop=(k == KD - 1))
                last.then_inc(w1_used, 1)

            pe.wait_ge(pooled, 1)
            pe.wait_ge(consts_landed, 16 * 6)
            for g in range(NG):
                last = mm(psum[:, g, 0:T], pool_f[:, g, :], p_t[:, g, :], start=True, stop=True)
            last.then_inc(z_pool_ready, 1)

            pe.wait_ge(z_ready, 2)
            pe.wait_ge(w_out_landed, 16)
            for t in range(NTILE):
                for n in range(YN):
                    for k in range(KD):
                        last = mm(psum[0:rows[t], (4 + YN * t + n) % 8, :], z_t[:, k, t * P:t * P + rows[t]],
                                  w_out_sb[:, k, n * BANK:(n + 1) * BANK], start=(k == 0), stop=(k == KD - 1))
                    last.then_inc(mixed, 1)

            for k in range(KD):
                for t in range(NTILE):
                    if k == 0:
                        pe.wait_ge(residual, YN * NTILE)
                    last = nc.tensor.transpose(psum[:, k, t * P:t * P + rows[t]],
                                               x_acc[0:rows[t], t, k * P:(k + 1) * P],
                                               ident[0:rows[t], 0:rows[t]])
                last.then_inc(x_t_ready, 1)
            pe.wait_ge(x_t_dve, KD)
            pe.wait_ge(x_t_act, KD)
            for t in range(NTILE):
                for k in range(KD):
                    last = mm(psum[0:rows[t], 0, t * E:(t + 1) * E], x_t[:, k, t * P:t * P + rows[t]],
                              router_g[:, k, :], start=(k == 0), stop=(k == KD - 1))
            last.then_inc(logits_ready, 1)

            pe.wait_ge(last_ready, 1)
            for j in range(KC):
                nc.tensor.transpose(psum[0:CB, 4, j * P:(j + 1) * P], u_pad[:, j, NP:NP + CB], ident[:])
                nc.tensor.transpose(psum[0:NB * CB, 5, j * P:(j + 1) * P], u_last[:, j, :], ident[:])
                nc.tensor.transpose(psum[0:PB, 6, j * P:(j + 1) * P], v_pad[:, j, NP:NP + PB], ident[:])
                last = nc.tensor.transpose(psum[0:NS, 7, j * P:(j + 1) * P], v_last[:, j, :], ident[:])
            last.then_inc(cache_ready, 1)
            pe.wait_ge(mask_ready, 1)
            for t in range(NTILE + 1):
                for s in range(min(t, NTILE - 1) + 1):
                    last = mm(psum[:, 1, t * E:(t + 1) * E], before[:] if s == t else ones[:], mask[:, s, :],
                              start=(s == 0), stop=(s == min(t, NTILE - 1)))
            last.then_inc(ranks_ready, 1)
            pe.wait_ge(combine_ready, 1)
            for t in range(NTILE):
                last = nc.tensor.transpose(psum[0:E, 2, t * P:t * P + rows[t]], combine[0:rows[t], t, 0:E],
                                           ident[0:rows[t], 0:rows[t]])
            last.then_inc(combine_t_ready, 1)

            def gather():
                for k in range(KD):
                    for t in range(NTILE):
                        last = mm(psum[:, 4 + k // 4, (k % 4) * P:(k % 4 + 1) * P],
                                  x_norm[0:rows[t], t, k * P:(k + 1) * P], place[0:rows[t], t],
                                  start=(t == 0), stop=(t == NTILE - 1))
                last.then_inc(gathered, 1)

            def turn_back():
                for t in range(NTILE):
                    last = nc.tensor.transpose(psum[:, 6, t * P:t * P + rows[t]], gated[0:rows[t], t],
                                               ident[0:rows[t], 0:rows[t]])
                last.then_inc(back_ready, 1)

            pe.wait_ge(combine_t_read, 1)
            pe.wait_ge(cache_read, 1)
            for t in range(NTILE):
                for n in range(YN):
                    last = mm(psum[0:rows[t], (3 + YN * t + n) % 8, :],
                              combine_t[:, t * P:t * P + rows[t]], b2_rows[:, n * BANK:(n + 1) * BANK],
                              start=True, stop=True)
            last.then_inc(b2_ready, 1)
            pe.wait_ge(b2_added, 1)

            def round_of(r):
                q0 = reg(nc.tensor, r * (PAIRS + 1), ROUNDS * (PAIRS + 1))
                if not isinstance(r, int):
                    pe.wait_ge(back_read, q0)
                    pe.wait_ge(y_read, 2 * PAIRS * r + 2)
                pe.wait_ge(slots_ready, q0 + 1)
                gather()
                turn_back()
                with nc.tensor.Fori(0, PAIRS) as pair:
                    n = reg(nc.tensor, r * PAIRS + pair, ROUNDS * PAIRS)
                    q = reg(nc.tensor, r * (PAIRS + 1) + pair, ROUNDS * (PAIRS + 1))
                    for c in range(W1N):
                        last = mm(psum[:, c, :], pick_b1[:], b1_rows[:, c * BANK:(c + 1) * BANK],
                                  start=True, stop=False, skip_group_check=True)
                    last.then_inc(bias_added, 1)
                    pe.wait_ge(gathered_read, 2 * q + 2)
                    for k in range(KD):
                        pe.wait_ge(w1_landed[k % 4], 32 * n + 16 * (k // 4) + 16)
                        for c in range(W1N):
                            for e in range(2):
                                last = mm(psum[e * SLOTS:(e + 1) * SLOTS, c, :], gathered_t[:, k, e, :],
                                          w1_ring[:, k % 4, e, c * BANK:(c + 1) * BANK],
                                          start=False, stop=(k == KD - 1), skip_group_check=True)
                        last.then_inc(w1_used, 1)
                    pe.wait_ge(slots_ready, q + 2)
                    pe.wait_ge(y_read, 2 * n + 2)
                    gather()
                    pe.wait_ge(back_read, q + 1)
                    pe.wait_ge(spread_read, 6 * n + 6)
                    for half_h in range(2):
                        pe.wait_ge(h_ready, 2 * n + half_h + 1)
                        for k in range(4):
                            last = nc.tensor.transpose(psum[:, 6 + half_h, k * P:(k + 1) * P],
                                                       hidden[:, 0, half_h, k * P:(k + 1) * P], ident[:])
                        last.then_inc(h_t_ready, 1)
                    pe.wait_ge(gathered_read, 2 * q + 4)
                    for k in range(KD):
                        if k % 4 == 0:
                            pe.wait_ge(h_t_read, 2 * n + k // 4 + 1)
                        if k % 2 == 0:
                            pe.wait_ge(w2_landed[k // 2], 32 * n + 32)
                        for c in range(YN):
                            for e in range(2):
                                last = mm(psum[e * SLOTS:(e + 1) * SLOTS, 4 + c, :], h_t[:, k, e, :],
                                          w2_ring[:, k // 2, e, k % 2, c * BANK:(c + 1) * BANK],
                                          start=(k == 0), stop=(k == KD - 1))
                        if k % 2 == 1:
                            last.then_inc(w2_used, 1)
                    for j in range(NTILE * YN):
                        t, c = divmod(j, YN)
                        if j < YN:
                            pe.wait_ge(y_read, 2 * n + 3 + c)
                        else:
                            pe.wait_ge(spread_read, 6 * n + 5 + j)
                        last = mm(psum[0:rows[t], 6 + j % 2, :], back[:, t * P:t * P + rows[t]],
                                  y_slots[:, c, :], start=True, stop=True)
                        last.then_inc(spread, 1)
                    pe.wait_ge(spread_read, 6 * n + 11)
                    turn_back()

            round_of(0)
            pe.wait_ge(counts_ready, 1)
            rounds_after_first(nc.tensor, round_of)

        @block.scalar
        def _(act):
            A = nc.scalar.activation

            for src, at_row in ((norm_mix_g[0].rearrange("(k c) -> k c", c=P), G_MIX),
                                (conv_w[0].rearrange("w (k c) -> (w k) c", c=P), CONV_W),
                                (pool_scale[0].rearrange("(k c) -> k c", c=P), SCALE),
                                (norm_ffn_g[0].rearrange("(k c) -> k c", c=P), G_FFN)):
                nc.scalar.dma_start(vec_rows[at_row:at_row + src.shape[0], :], src).then_inc(vecs_landed, 16)
            nc.scalar.dma_start(conv_rows, state_conv[0].rearrange("b j c -> (b j) c")).then_inc(states_landed, 16)
            nc.scalar.dma_start(pool_rows[:], state_pool[0].rearrange("b j c -> (b j) c")).then_inc(states_landed, 16)
            act.wait_ge(presets_made, 1)
            for t in range(NTILE):
                act.wait_ge(x_landed[t], 16)
                A(x_norm[0:rows[t], t, :], x_acc[0:rows[t], t, :], ACT.Square,
                  accum_out=sumsq[0:rows[t], 0, t:t + 1]).then_inc(squares, 1)
            nc.scalar.dma_start(router_f[:], router_w[0].rearrange("(k p) e -> p k e", p=P)).then_inc(consts_landed, 16)
            nc.scalar.dma_start(bias_e[:], router_b.to_broadcast([P, E])).then_inc(consts_landed, 16)
            nc.scalar.dma_start(pool_f[:], pool_w[0].rearrange("g c d -> c g d")).then_inc(consts_landed, 16)
            nc.scalar.dma_start(g_ffn[:], norm_ffn_g.to_broadcast([P, D])).then_inc(consts_landed, 16)
            nc.scalar.dma_start(b1_rows[:], exp_b1[0]).then_inc(consts_landed, 16)
            nc.scalar.dma_start(b2_rows[:], exp_b2[0]).then_inc(consts_landed, 16)
            nc.scalar.dma_start(new_pool_sample[0][:, 0:PB - NT, :], state_pool[0][:, NT:PB, :]).then_inc(stored, 16)

            act.wait_ge(rms_ready, 1)
            act.wait_ge(squares, NTILE)
            A(x_norm[:, 1, :], x_acc[:, 1, :], ACT.Copy, scale=rms[:, 0, 1:2]).then_inc(scaled, 1)
            act.wait_ge(front_t_read, 3)
            for k in range(1, KD, 2):
                act.wait_ge(x_t_ready, k + 1)
                A(x_t[:, k, :], psum[:, k, 0:T], ACT.Copy, scale=vecs[:, G_MIX + k:G_MIX + k + 1]).then_inc(x_t_act, 1)
            act.wait_ge(w1_used, 1)
            A(c_gate, psum[:, 0:4, 0:T], ACT.Copy).then_inc(proj_read, 1)
            act.wait_ge(w1_used, 3)
            act.wait_ge(front_t_read, 5)
            A(v_pad[:, :, PB:PB + NP], psum[:, 0:4, 0:NP], ACT.Copy)
            for j in range(NG):
                last = A(v_pad[:, j, PS:PL].rearrange("p (b t) -> p b t", b=NB)[:, :, PB:PB + NT],
                         psum[:, j, NP:T].rearrange("p (b t) -> p b t", b=NB), ACT.Copy)
            last.then_inc(v_ready, 1)
            act.wait_ge(z_pool_ready, 1)
            for g in range(NG):
                last = A(z_t[:, KC + g, :], psum[:, g, 0:T], ACT.Copy, scale=vecs[:, SCALE + g:SCALE + g + 1])
            last.then_inc(z_ready, 1)
            for t in range(NTILE):
                act.wait_ge(residual, YN * (t + 1))
                A(x_norm[0:rows[t], t, :], x_acc[0:rows[t], t, :], ACT.Square,
                  accum_out=sumsq[0:rows[t], 1, t:t + 1]).then_inc(squares, 1)
            for k in range(1, KD, 2):
                act.wait_ge(x_t_ready, KD + k + 1)
                A(x_t[:, k, :], psum[:, k, 0:T], ACT.Copy).then_inc(x_t_act, 1)
            act.wait_ge(shifted_ready, 1)
            A(shifted[:], shifted[:], ACT.Exp).then_inc(exp_ready, 1)
            act.wait_ge(cache_ready, 1)
            A(cache_rows[0:CB, 0, :], psum[0:CB, 4, :], ACT.Copy)
            A(cache_rows[0:NB * CB, 1, :], psum[0:NB * CB, 5, :], ACT.Copy)
            A(cache_rows[0:PB, 2, :], psum[0:PB, 6, :], ACT.Copy)
            A(cache_rows[0:NS, 3, :], psum[0:NS, 7, :], ACT.Copy).then_inc(cache_read, 1)
            act.wait_ge(cache_read, 1)
            nc.scalar.dma_start(new_conv_prompt[0, 0], cache_rows[0:CB, 0, :]).then_inc(cache_stored, 16)
            nc.scalar.dma_start(new_conv_sample[0].rearrange("b j c -> (b j) c"),
                                cache_rows[0:NB * CB, 1, :]).then_inc(cache_stored, 16)
            nc.scalar.dma_start(new_pool_prompt[0, 0], cache_rows[0:PB, 2, :]).then_inc(cache_stored, 16)
            for b in range(NB):
                nc.scalar.dma_start(new_pool_sample[0, b, PB - NT:PB, :],
                                    cache_rows[b * NT:(b + 1) * NT, 3, :]).then_inc(cache_stored, 16)
            act.wait_ge(combine_t_ready, 1)
            A(combine_t[:], psum[0:E, 2, 0:T], ACT.Copy).then_inc(combine_t_read, 1)
            act.wait_ge(b2_added, 1)
            nc.scalar.sem_inc(y_read, 2)
            act.wait_ge(cache_stored, 16 * (3 + NB))
            nc.scalar.sem_inc(w2_used, 4)

            def copy_gathered(q):
                act.wait_ge(gathered, q + 1)
                for b in range(2):
                    A(routed[:, 0, b * BANK:(b + 1) * BANK], psum[:, 4 + b, :], ACT.Copy).then_inc(gathered_read, 1)

            def copy_back(q):
                act.wait_ge(back_ready, q + 1)
                A(back[:], psum[:, 6, 0:T], ACT.Copy).then_inc(back_read, 1)

            def round_of(r):
                q0 = reg(nc.scalar, r * (PAIRS + 1), ROUNDS * (PAIRS + 1))
                copy_gathered(q0)
                copy_back(q0)
                with nc.scalar.Fori(0, PAIRS) as pair:
                    n = reg(nc.scalar, r * PAIRS + pair, ROUNDS * PAIRS)
                    q = reg(nc.scalar, r * (PAIRS + 1) + pair, ROUNDS * (PAIRS + 1))
                    for b in range(2):
                        act.wait_ge(gate_ready, 2 * n + b + 1)
                        A(hidden[:, 2, b, :], hidden[:, 0, b, :], ACT.Sigmoid, scale=SWIGLU_ALPHA).then_inc(sig_ready, 1)
                    copy_gathered(q + 1)
                    for b in range(2):
                        act.wait_ge(h_t_ready, 2 * n + b + 1)
                        A(routed[:, 1, b * BANK:(b + 1) * BANK], psum[:, 6 + b, :], ACT.Copy).then_inc(h_t_read, 1)
                    act.wait_ge(w2_used, 4 * n + 8)
                    for c in range(YN):
                        A(y_slots[:, c, :], psum[:, 4 + c, :], ACT.Copy).then_inc(y_read, 1)
                    copy_back(q + 1)

            round_of(0)
            act.wait_ge(counts_ready, 1)
            rounds_after_first(nc.scalar, round_of)

            act.wait_ge(moe_done, 1)
            nc.scalar.dma_start(g_final, final_norm_g[None, :].to_broadcast([P, D])).then_inc(g_final_landed, 16)
            for t in range(NTILE):
                A(x_norm[0:rows[t], t, :], x_acc[0:rows[t], t, :], ACT.Square,
                  accum_out=sumsq[0:rows[t], 2, t:t + 1]).then_inc(squares, 1)

        @block.vector
        def _(dve):
            V = nc.vector
            step = Counter(dve_step)

            def then(ins):
                step.inc(ins)
                dve.wait_ge(dve_step, step.now())

            V.memset(sumsq[:], 1.0)
            V.memset(half[:], -0.5)
            V.memset(logits[:], 0.0)
            V.memset(rank[:], -1.0)
            V.memset(combine[:], 0.0).then_inc(presets_made, 1)
            dve.wait_ge(presets_made, 1)
            dve.wait_ge(front_t, 1)
            V.tensor_copy(vecs[:], psum[:, 0, 0:4 * KD]).then_inc(front_t_read, 1)
            dve.wait_ge(front_t, 3)
            for j in range(KC):
                last = V.tensor_copy(u_pad[:, j, CS:CL].rearrange("p (b t) -> p b t", b=NB)[:, :, 0:CB],
                                     psum[:, 1, 16 * j:16 * j + NB * CB].rearrange("p (b t) -> p b t", b=NB))
            last.then_inc(front_t_read, 1)
            for j in range(NG):
                last = V.tensor_copy(v_pad[:, j, PS:PL].rearrange("p (b t) -> p b t", b=NB)[:, :, 0:PB],
                                     psum[:, 2, P * j:P * j + NB * PB].rearrange("p (b t) -> p b t", b=NB))
            last.then_inc(front_t_read, 1)
            dve.wait_ge(rms_ready, 1)
            for t in (0, 2):
                last = V.tensor_scalar(x_norm[0:rows[t], t, :], x_acc[0:rows[t], t, :], rms[0:rows[t], 0, t:t + 1],
                                       None, ALU.mult)
                last.then_inc(scaled, 1)
            V.memset(u_pad[:, :, 0:CB], 0.0).then_inc(front_t_read, 1)
            V.memset(v_pad[:, :, 0:PB], 0.0).then_inc(front_t_read, 1)
            dve.wait_ge(front_t_read, 5)
            for k in range(0, KD, 2):
                dve.wait_ge(x_t_ready, k + 1)
                V.tensor_scalar(x_t[:, k, :], psum[:, k, 0:T], vecs[:, G_MIX + k:G_MIX + k + 1], None,
                                ALU.mult).then_inc(x_t_dve, 1)
            dve.wait_ge(consts_made, 2)
            then(V.reciprocal(ramp[:], ramp[:]))
            for g, w in enumerate(WINDOWS):
                last = V.tensor_scalar(fix[:, g, :], ramp[:], float(w), 1.0, ALU.mult, ALU.max)
            dve.wait_ge(consts_landed, 16 * 6)
            for k in range(KD):
                last = V.tensor_scalar(router_g[:, k, :], router_f[:, k, :], vecs[:, G_FFN + k:G_FFN + k + 1], None,
                                       ALU.mult)
            then(last)

            dve.wait_ge(proj_read, 1)
            dve.wait_ge(w1_used, 2)
            V.tensor_tensor(u_pad[:, :, CB:CB + NP], psum[:, 4:8, 0:NP], c_gate[:, :, 0:NP], ALU.mult)
            for j in range(KC):
                last = V.tensor_tensor(u_pad[:, j, CS:CL].rearrange("p (b t) -> p b t", b=NB)[:, :, CB:CB + NT],
                                       psum[:, 4 + j, NP:T].rearrange("p (b t) -> p b t", b=NB),
                                       c_gate[:, j, NP:T].rearrange("p (b t) -> p b t", b=NB), ALU.mult)
            last.then_inc(proj_read, 1)
            dve.wait_ge(proj_read, 2)
            for w in range(3):
                for j in range(KC):
                    wcol = vecs[:, CONV_W + KC * w + j:CONV_W + KC * w + j + 1]
                    src = u_pad[:, j, w:w + CY]
                    if w == 0:
                        last = V.tensor_scalar(conv_y[:, j, 0:CY], src, wcol, None, ALU.mult)
                    else:
                        last = V.scalar_tensor_tensor(out=conv_y[:, j, 0:CY], in0=src, scalar=wcol,
                                                      in1=conv_y[:, j, 0:CY], op0=ALU.mult, op1=ALU.add)
                then(last)
            dve.wait_ge(v_ready, 1)
            then(V.tensor_tensor(sum_a[:, :, 1:PL], v_pad[:, :, 1:PL], v_pad[:, :, 0:PL - 1], ALU.add))
            then(V.tensor_tensor(sum_b[:, 1:4, 3:PL], sum_a[:, 1:4, 3:PL], sum_a[:, 1:4, 1:PL - 2], ALU.add))
            then(V.tensor_tensor(sum_a[:, 2:4, 7:PL], sum_b[:, 2:4, 7:PL], sum_b[:, 2:4, 3:PL - 4], ALU.add))
            then(V.tensor_tensor(sum_b[:, 3, 15:PL], sum_a[:, 3, 15:PL], sum_a[:, 3, 7:PL - 8], ALU.add))
            sums = (sum_a, sum_b, sum_a, sum_b)
            for g in range(NG):
                last = V.tensor_tensor(sums[g][:, g, PB:PB + 16], sums[g][:, g, PB:PB + 16], fix[:, g, :], ALU.mult)
            then(last)
            for g, w in enumerate(WINDOWS):
                V.scalar_tensor_tensor(out=p_t[:, g, 0:NP], in0=sums[g][:, g, PB:PB + NP], scalar=1.0 / w,
                                       in1=v_pad[:, g, PB:PB + NP], op0=ALU.mult, op1=ALU.subtract)
                tail_s = sums[g][:, g, PS:PL].rearrange("p (b t) -> p b t", b=NB)[:, :, PB:PB + NT]
                tail_v = v_pad[:, g, PS:PL].rearrange("p (b t) -> p b t", b=NB)[:, :, PB:PB + NT]
                last = V.scalar_tensor_tensor(out=p_t[:, g, NP:T].rearrange("p (b t) -> p b t", b=NB), in0=tail_s,
                                              scalar=1.0 / w, in1=tail_v, op0=ALU.mult, op1=ALU.subtract)
            last.then_inc(pooled, 1)
            dve.wait_ge(w1_used, 4)
            V.tensor_tensor(z_t[:, 0:KC, 0:NP], psum[:, 4:8, 0:NP], conv_y[:, :, 0:NP], ALU.mult)
            for j in range(KC):
                last = V.tensor_tensor(z_t[:, j, NP:T].rearrange("p (b t) -> p b t", b=NB),
                                       psum[:, 4 + j, NP:T].rearrange("p (b t) -> p b t", b=NB),
                                       conv_y[:, j, CS:CL].rearrange("p (b t) -> p b t", b=NB)[:, :, 0:NT], ALU.mult)
            last.then_inc(z_ready, 1)
            dve.wait_ge(pooled, 1)
            V.tensor_copy(u_last.rearrange("p k (b t) -> p k b t", b=NB),
                          u_pad[:, :, CS:CL].rearrange("p k (b t) -> p k b t", b=NB)[:, :, :, NT:NT + CB])
            V.tensor_copy(v_last.rearrange("p k (b t) -> p k b t", b=NB),
                          v_pad[:, :, PS:PL].rearrange("p k (b t) -> p k b t", b=NB)[:, :, :, PB:PB + NT]).then_inc(last_ready, 1)
            for t in range(NTILE):
                for n in range(YN):
                    dve.wait_ge(mixed, YN * t + n + 1)
                    V.tensor_tensor(x_acc[0:rows[t], t, n * BANK:(n + 1) * BANK],
                                    x_acc[0:rows[t], t, n * BANK:(n + 1) * BANK],
                                    psum[0:rows[t], (4 + YN * t + n) % 8, :], ALU.add).then_inc(residual, 1)
            for k in range(0, KD, 2):
                dve.wait_ge(x_t_ready, KD + k + 1)
                V.tensor_copy(x_t[:, k, :], psum[:, k, 0:T]).then_inc(x_t_dve, 1)

            dve.wait_ge(rms_ready, 2)
            dve.wait_ge(logits_ready, 1)
            for t in range(NTILE):
                last = V.scalar_tensor_tensor(out=logits[0:rows[t], t, :], in0=psum[0:rows[t], 0, t * E:(t + 1) * E],
                                              scalar=rms[0:rows[t], 1, t:t + 1], in1=bias_e[0:rows[t], :],
                                              op0=ALU.mult, op1=ALU.add)
            then(last)
            for t in range(NTILE):
                last = V.max(top8[:, t, :], logits[:, t, :])
            then(last)
            V.tensor_tensor(shifted[:], logits[:], top8[:, :, 0:1].to_broadcast([P, NTILE, E]),
                            ALU.subtract).then_inc(shifted_ready, 1)
            for t in range(NTILE):
                last = V.max_index(top_at[:, t, :], top8[:, t, :], logits[:, t, :])
            then(last)
            then(V.tensor_copy(top_f[:], top_at[:]))
            dve.wait_ge(consts_made, 2)
            for t in range(NTILE):
                last = V.tensor_tensor(match[:, t], expert_id[:].unsqueeze(2).to_broadcast([P, E, TOP_K]),
                                       top_f[:, t, 0:TOP_K].unsqueeze(1).to_broadcast([P, E, TOP_K]), ALU.is_equal)
            then(last)
            then(V.tensor_reduce(mask[:], match[:], AX.X, ALU.max))
            V.memset(mask[32:64, 2, :], 0.0)
            V.memset(mask[64:128, 2, :], 0.0).then_inc(mask_ready, 1)
            dve.wait_ge(mask_ready, 1)
            dve.wait_ge(exp_ready, 1)
            then(V.tensor_tensor(combine[:, :, 0:E], shifted[:], mask[:], ALU.mult))
            then(V.tensor_reduce(denom[:], combine[:, :, 0:E], AX.X, ALU.add))
            V.memset(denom[32:64, 2:3], 1.0)
            then(V.memset(denom[64:128, 2:3], 1.0))
            then(V.reciprocal(denom[:], denom[:]))
            V.tensor_tensor(combine[:, :, 0:E], combine[:, :, 0:E], denom[:].unsqueeze(2).to_broadcast([P, NTILE, E]),
                            ALU.mult).then_inc(combine_ready, 1)
            dve.wait_ge(combine_ready, 1)
            dve.wait_ge(ranks_ready, 1)
            V.reduce_max(most[:], psum[:, 1, NTILE * E:(NTILE + 1) * E], AX.X)
            then(V.scalar_tensor_tensor(out=rank[:, :, 0:E],
                                        in0=psum[:, 1, 0:NTILE * E].rearrange("p (t e) -> p t e", t=NTILE),
                                        scalar=1.0, in1=mask[:], op0=ALU.add, op1=ALU.mult))
            V.tensor_copy(most_i[:], most[:]).then_inc(counts_ready, 1)
            then(V.tensor_scalar(rank[:, :, 0:E], rank[:, :, 0:E], -1.0, None, ALU.add))
            dve.wait_ge(squares, 2 * NTILE)
            for t in range(NTILE):
                last = V.scalar_tensor_tensor(out=x_norm[0:rows[t], t, :], in0=x_acc[0:rows[t], t, :],
                                              scalar=rms[0:rows[t], 1, t:t + 1], in1=g_ffn[0:rows[t], :],
                                              op0=ALU.mult, op1=ALU.mult)
            then(last)
            dve.wait_ge(b2_ready, 1)
            for t in range(NTILE):
                for n in range(YN):
                    last = V.tensor_tensor(x_acc[0:rows[t], t, n * BANK:(n + 1) * BANK],
                                           x_acc[0:rows[t], t, n * BANK:(n + 1) * BANK],
                                           psum[0:rows[t], (3 + YN * t + n) % 8, :], ALU.add)
            last.then_inc(b2_added, 1)
            dve.wait_ge(b2_added, 1)
            dve.sem_inc(spread_read, NTILE * YN)

            def build(pair, q):
                def own(table):
                    return table[:, :, bass.ds(pair * 2, 2)].unsqueeze(3).to_broadcast([P, NTILE, 2, SLOTS])

                ids = slot_id[:].unsqueeze(1).unsqueeze(1).to_broadcast([P, NTILE, 2, SLOTS])
                V.tensor_tensor(place[:], ids, own(rank), ALU.is_equal).then_inc(dve_build, 1)
                V.tensor_copy(pick_b1[:], ident[0:E, bass.ds(pair * 2, 2)].unsqueeze(2).to_broadcast([E, 2, SLOTS]))
                dve.wait_ge(dve_build, q + 1)
                V.tensor_tensor(gated[:], place[:], own(combine), ALU.mult).then_inc(slots_ready, 1)

            def round_of(r):
                q0 = reg(nc.vector, r * (PAIRS + 1), ROUNDS * (PAIRS + 1))
                if not isinstance(r, int):
                    dve.wait_ge(back_ready, q0)
                    V.tensor_scalar(slot_id[:], slot_id[:], float(SLOTS), None, ALU.add).then_inc(slot_step, 1)
                    dve.wait_ge(slot_step, r)
                build(0, q0)
                with nc.vector.Fori(0, PAIRS) as pair:
                    n = reg(nc.vector, r * PAIRS + pair, ROUNDS * PAIRS)
                    q = reg(nc.vector, r * (PAIRS + 1) + pair, ROUNDS * (PAIRS + 1))
                    nxt = reg(nc.vector, pair + 1, PAIRS)
                    dve.wait_ge(bias_added, n + 1)
                    build(nxt, q + 1)
                    dve.wait_ge(w1_used, KD * n + KD + 4)
                    for b in range(2):
                        V.tensor_scalar(hidden[:, 0, b, :], psum[:, b, :], SWIGLU_LIMIT, None,
                                        ALU.min).then_inc(gate_ready, 1)
                    for b in range(2):
                        V.tensor_scalar(hidden[:, 1, b, :], psum[:, 2 + b, :], SWIGLU_LIMIT, -SWIGLU_LIMIT,
                                        ALU.min, ALU.max).then_inc(lin_step, 1)
                    dve.wait_ge(gate_ready, 2 * n + 2)
                    for b in range(2):
                        dve.wait_ge(lin_step, 4 * n + b + 1)
                        V.scalar_tensor_tensor(out=hidden[:, 1, b, :], in0=hidden[:, 1, b, :], scalar=1.0,
                                               in1=hidden[:, 0, b, :], op0=ALU.add, op1=ALU.mult).then_inc(lin_step, 1)
                    for b in range(2):
                        dve.wait_ge(lin_step, 4 * n + 3 + b)
                        dve.wait_ge(sig_ready, 2 * n + b + 1)
                        V.tensor_tensor(hidden[:, 0, b, :], hidden[:, 1, b, :], hidden[:, 2, b, :],
                                        ALU.mult).then_inc(h_ready, 1)
                    for j in range(NTILE * YN):
                        t, c = divmod(j, YN)
                        dve.wait_ge(spread, 6 * n + j + 1)
                        V.tensor_tensor(x_acc[0:rows[t], t, c * BANK:(c + 1) * BANK],
                                        x_acc[0:rows[t], t, c * BANK:(c + 1) * BANK],
                                        psum[0:rows[t], 6 + j % 2, :], ALU.add).then_inc(spread_read, 1)

            round_of(0)
            dve.wait_ge(counts_ready, 1)
            rounds_after_first(nc.vector, round_of)
            V.memset(most[:], 0.0).then_inc(moe_done, 1)

            dve.wait_ge(rms_ready, 3)
            dve.wait_ge(squares, 3 * NTILE)
            dve.wait_ge(g_final_landed, 16)
            for t in range(NTILE):
                V.scalar_tensor_tensor(out=x_norm[0:rows[t], t, :], in0=x_acc[0:rows[t], t, :],
                                       scalar=rms[0:rows[t], 2, t:t + 1], in1=g_final[0:rows[t], :],
                                       op0=ALU.mult, op1=ALU.mult).then_inc(final_ready, 1)

        @block.gpsimd
        def _(pool):
            G = nc.gpsimd
            G.memset(ident[:], 0.0)
            G.memset(ones[:], 1.0).then_inc(pool_step, 1)
            pool.wait_ge(pool_step, 1)
            G.affine_select(out=ident[:], in_=ident[:], compare_op=ALU.not_equal, fill=1.0, base=0,
                            pattern=[[-1, P]], channel_multiplier=1).then_inc(consts_made, 1)
            G.affine_select(out=before[:], in_=ones[:], compare_op=ALU.is_ge, fill=0.0, base=-1,
                            pattern=[[1, P]], channel_multiplier=-1)
            G.iota(slot_id[:], pattern=[[1, SLOTS]], base=0, channel_multiplier=0, allow_small_or_imprecise_dtypes=True)
            G.iota(expert_id[:], pattern=[[1, E]], base=0, channel_multiplier=0, allow_small_or_imprecise_dtypes=True)
            G.iota(ramp[:], pattern=[[1, 16]], base=1, channel_multiplier=0,
                   allow_small_or_imprecise_dtypes=True).then_inc(consts_made, 1)
            pool.wait_ge(presets_made, 1)
            for i in range(3):
                if i == 2:
                    pool.wait_ge(moe_done, 1)
                pool.wait_ge(squares, NTILE * (i + 1))
                G.tensor_scalar(rms[:, i, :], sumsq[:, i, :], 1.0 / D, EPS, ALU.mult, ALU.add).then_inc(pool_step, 1)
                pool.wait_ge(pool_step, 2 + i)
                G.tensor_tensor(rms[:, i, :], rms[:, i, :], half[:], ALU.pow).then_inc(rms_ready, 1)


INPUTS = ["x_prompt", "x_sample", "state_conv", "state_pool", "norm_mix_g", "w_in", "conv_w", "pool_w",
          "pool_scale", "w_out", "norm_ffn_g", "router_w", "router_b", "exp_w1", "exp_b1", "exp_w2",
          "exp_b2", "final_norm_g"]


def kernel(**inputs):
    import numpy as np
    import concourse.bacc as bacc
    from concourse.bass_utils import run_bass_kernel_spmd

    nc = bacc.Bacc("TRN2", target_bir_lowering=False, num_devices=1)
    arrays, aps = {}, []
    for name in INPUTS:
        a = np.ascontiguousarray(inputs[name])
        arrays[f"in_{name}"] = a
        aps.append(nc.dram_tensor(f"in_{name}", a.shape, mybir.dt.from_np(a.dtype), kind="ExternalInput").ap())
    xp, xs, sc, sp = (inputs[n].shape for n in ("x_prompt", "x_sample", "state_conv", "state_pool"))
    shapes = [xp, xs, (sc[0], xp[0]) + tuple(sc[2:]), (sp[0], xp[0]) + tuple(sp[2:]), sc, sp]
    for i, shape in enumerate(shapes):
        aps.append(nc.dram_tensor(f"out_{i}", tuple(shape), F32, kind="ExternalOutput").ap())
    hybrid_moe_layer(nc, *aps)
    results = run_bass_kernel_spmd(nc, [arrays], core_ids=[0]).results[0]
    return tuple(results[f"out_{i}"] for i in range(len(shapes)))
```

```python
from contextlib import ExitStack

import concourse.bass as bass
from concourse import mybir

F32 = mybir.dt.float32
F32R = mybir.dt.float32r
I32 = mybir.dt.int32
U32 = mybir.dt.uint32
ALU = mybir.AluOpType
ACT = mybir.ActivationFunctionType
AX = mybir.AxisListType

P = 128
BANK = 512
SWIGLU_LIMIT = 7.0
SWIGLU_ALPHA = 1.702
EPS = 1e-5
TOP_K = 4
WINDOWS = (2, 4, 8, 16)
SLOTS = 64
W2_EARLY = (4, 3, 2, 1)


class Counter:

    def __init__(self, sem):
        self.sem, self.base, self.n = sem, 0, 0

    def inc(self, instruction, by=1):
        instruction.then_inc(self.sem, by)
        self.n += by

    def now(self):
        return self.base + self.n


def hybrid_moe_layer(nc, x_prompt, x_sample, state_conv, state_pool, norm_mix_g, w_in, conv_w,
                     pool_w, pool_scale, w_out, norm_ffn_g, router_w, router_b, exp_w1, exp_b1,
                     exp_w2, exp_b2, final_norm_g, y_prompt, y_sample, new_conv_prompt,
                     new_pool_prompt, new_conv_sample, new_pool_sample):
    _, NP, D = x_prompt.shape
    NB, NT, _ = x_sample.shape
    NS = NB * NT
    T = NP + NS
    DC, DPL = state_conv.shape[3], state_pool.shape[3]
    CB, PB = state_conv.shape[2], state_pool.shape[2]
    E = router_w.shape[2]
    F = exp_w2.shape[2]
    KD = D // P
    KC = DC // P
    NTILE = (T + P - 1) // P
    rows = [min(P, T - P * t) for t in range(NTILE)]
    NG = len(WINDOWS)
    PAIRS = E // 2
    ROUNDS = (T + SLOTS - 1) // SLOTS
    W1N = 2 * F // BANK
    YN = D // BANK
    assert NP == 2 * P and NS == 32 and D == F and DC == DPL and KC == NG and D % BANK == 0

    CL = CB + NP + NB * (CB + NT)
    PL = PB + NP + NB * (PB + NT)
    CS, PS = CB + NP, PB + NP
    CY = CL - CB

    ctx = ExitStack()
    with ctx:
        def sb(name, shape, dt=F32):
            return ctx.enter_context(nc.sbuf_tensor(name, shape, dt))

        def sem(name):
            return ctx.enter_context(nc.semaphore(name))

        w1_ring = sb("w1_ring", [P, 4, 2, 2 * F])
        w1_ring_at = nc.sbuf_base - 4 * 4 * 2 * 2 * F
        w2_ring = sb("w2_ring", [P, 4, 2, 2, D])
        x_acc = sb("x_acc", [P, NTILE, D])
        x_norm = sb("x_norm", [P, NTILE, D])
        work = sb("work", [P, 2, 3 * D])
        work_at = nc.sbuf_base - 4 * 2 * 3 * D
        hidden = work[:, 0, :].rearrange("p (a b n) -> p a b n", a=3, b=2)
        routed = work[:, 1, :].rearrange("p (a n) -> p a n", a=3)
        b1_rows = sb("b1_rows", [W1N * E, BANK])
        b2_rows = sb("b2_rows", [YN * E, BANK])
        gain = sb("gain", [P, D])
        back = sb("back", [P, T])
        place = sb("place", [P, NTILE, 2, SLOTS])
        gated = sb("gated", [P, NTILE, 2, SLOTS])
        pick_b1 = sb("pick_b1", [P, 2, SLOTS])
        pick_b2 = sb("pick_b2", [P, 2, SLOTS])
        pick_table = sb("pick_table", [P, E + 2])
        ident = sb("ident", [P, P])
        before = sb("before", [P, P])
        ones = sb("ones", [P, P])
        slot_id = sb("slot_id", [P, SLOTS])
        expert_id = sb("expert_id", [P, E])
        vec_rows = sb("vec_rows", [4 * KD, P])
        vecs = sb("vecs", [P, 4 * KD])
        router_f = sb("router_f", [P, KD, E])
        router_g = sb("router_g", [P, KD, E])
        bias_e = sb("bias_e", [P, E])
        pool_f = sb("pool_f", [P, NG, P])
        fix = sb("fix", [P, NG, 16])
        ramp = sb("ramp", [P, 16])
        warm = sb("warm", [P, 1])
        sumsq = sb("sumsq", [P, 3, NTILE])
        rms = sb("rms", [P, 3, NTILE])
        half = sb("half", [P, NTILE])
        logits = sb("logits", [P, NTILE, E])
        top8 = sb("top8", [P, NTILE, 8])
        top_at = sb("top_at", [P, NTILE, 8], U32)
        top_f = sb("top_f", [P, NTILE, 8])
        mask = sb("mask", [P, NTILE + 1, E])
        shifted = sb("shifted", [P, NTILE, E])
        combine = sb("combine", [P, NTILE, E + 2])
        rank = sb("rank", [P, NTILE, E + 2])
        denom = sb("denom", [P, NTILE])
        most = sb("most", [P, 1])
        most_i = sb("most_i", [P, 1], I32)
        psum = ctx.enter_context(nc.psum_tensor("psum", [P, 8, BANK], F32))

        w_in_sb = w1_ring[:].rearrange("p s e n -> p s (e n)").rearrange("p s (k n) -> p s k n", k=KD)
        w2_flat = w2_ring[:].rearrange("p s e k n -> p (s e k n)")
        w_out_sb = w2_flat[:, 0:KD * D].rearrange("p (k n) -> p k n", k=KD)
        at = KD * D

        def scratch(blocks, length):
            nonlocal at
            v = w2_flat[:, at:at + blocks * length].rearrange("p (k n) -> p k n", k=blocks)
            at += blocks * length
            return v

        u_pad = scratch(KC, CL)
        v_pad = scratch(NG, PL)
        sum_a = scratch(NG, PL)
        sum_b = scratch(NG, PL)
        conv_y = scratch(KC, CL)
        assert at <= 4 * 4 * D
        flat_h = work[:, 0, :]
        x_t = flat_h[:, 0:KD * T].rearrange("p (k n) -> p k n", k=KD)
        flat_r = work[:, 1, :]
        match = flat_h[:, KD * T:KD * T + NTILE * E * TOP_K].rearrange("p (t e k) -> p t e k", t=NTILE, k=TOP_K)
        z_conv = flat_r[:, 0:KC * T].rearrange("p (k n) -> p k n", k=KC)
        logit_parts = flat_r[:, 0:T]
        flat_n = x_norm[:].rearrange("p a n -> p (a n)")
        c_gate = flat_n[:, 0:KC * T].rearrange("p (k n) -> p k n", k=KC)
        p_t = c_gate
        z_pool = c_gate
        x_parts = nc.alloc_sbuf_tensor_at("x_parts", [P, 2, KD, T], F32R, offset=work_at)
        w_high = nc.alloc_sbuf_tensor_at("w_high", [P, 3, DC], F32R, offset=work_at + 4 * 2 * KD * T)
        assert 2 * KD * T + 3 * DC <= 2 * 3 * D
        w_low = nc.alloc_sbuf_tensor_at("w_low", [P, 4, KD, DC], F32R, offset=w1_ring_at)
        conv_rows = sum_a[0:NB * CB].rearrange("p k n -> p (k n)")[:, 0:DC]
        pool_rows = sum_b[0:NB * PB].rearrange("p k n -> p (k n)")[:, 0:DPL]
        cache_at = KC * T
        cache_rows = flat_n[:, cache_at:cache_at + 3 * DC].rearrange("p (k n) -> p k n", k=3)
        cache_rows_v = sb("cache_rows_v", [NS, DPL])
        last_at = cache_at + 3 * DC
        u_last = flat_n[:, last_at:last_at + KC * NB * CB].rearrange("p (k n) -> p k n", k=KC)
        v_last = flat_n[:, last_at + KC * NB * CB:last_at + KC * (NB * CB + NS)].rearrange("p (k n) -> p k n", k=NG)
        gathered_t = routed[:, 0, :].rearrange("p (k e s) -> p k e s", k=KD, e=2)
        h_t = routed[:, 1, :].rearrange("p (k e s) -> p k e s", k=KD, e=2)
        y_slots = routed[:, 2, :].rearrange("p (n c) -> p n c", n=YN)

        MIX_ORDER = (2, 0, 1)

        def mix_bank(t, n):
            return YN * MIX_ORDER.index(t) + n

        G_MIX, CONV_W, SCALE, G_FFN = 0, KD, KD + 3 * KC, 2 * KD + 2 * KC
        assert G_FFN == 3 * KD

        x_landed = [sem(f"x_landed{t}") for t in range(NTILE)]
        w_in_landed = [sem(f"w_in_landed{j}") for j in range(4)]
        w_out_landed = sem("w_out_landed")
        vecs_landed = sem("vecs_landed")
        states_landed = sem("states_landed")
        consts_landed = sem("consts_landed")
        w1_landed = [sem(f"w1_landed{s}") for s in range(4)]
        w2_landed = [sem(f"w2_landed{s}") for s in range(4)]
        g_final_landed = sem("g_final_landed")
        stored = sem("stored")
        dve_step = sem("dve_step")
        pool_step = sem("pool_step")
        consts_made = sem("consts_made")
        presets_made = sem("presets_made")
        v_ready = sem("v_ready")
        last_ready = sem("last_ready")
        cache_read = sem("cache_read")
        cache_stored = sem("cache_stored")
        squares = sem("squares")
        rms_ready = sem("rms_ready")
        scaled = sem("scaled")
        front_t = sem("front_t")
        front_t_read = sem("front_t_read")
        x_high_ready = sem("x_high_ready")
        x_low_ready = sem("x_low_ready")
        w_high_ready = sem("w_high_ready")
        w_low_ready = sem("w_low_ready")
        w_in_used = sem("w_in_used")
        x_t_ready = sem("x_t_ready")
        x_t_dve = sem("x_t_dve")
        x_t_act = sem("x_t_act")
        proj_read = sem("proj_read")
        u_ready = sem("u_ready")
        pooled = sem("pooled")
        z_pool_ready = sem("z_pool_ready")
        z_pool_scaled = sem("z_pool_scaled")
        z_ready = sem("z_ready")
        mixed = sem("mixed")
        residual = sem("residual")
        logit_parts_ready = sem("logit_parts_ready")
        logit_parts_read = sem("logit_parts_read")
        logits_ready = sem("logits_ready")
        cache_ready = sem("cache_ready")
        shifted_ready = sem("shifted_ready")
        exp_ready = sem("exp_ready")
        mask_ready = sem("mask_ready")
        ranks_ready = sem("ranks_ready")
        combine_ready = sem("combine_ready")
        w_out_used = sem("w_out_used")
        x_norm_ready = sem("x_norm_ready")
        counts_ready = sem("counts_ready")
        w1_used = sem("w1_used")
        y_part = sem("y_part")
        w2_used = sem("w2_used")
        slots_ready = sem("slots_ready")
        gathered = sem("gathered")
        gathered_read = sem("gathered_read")
        back_ready = sem("back_ready")
        back_read = sem("back_read")
        picked_b1 = sem("picked_b1")
        picked_b2 = sem("picked_b2")
        dve_build = sem("dve_build")
        slot_step = sem("slot_step")
        lin_step = sem("lin_step")
        moe_done = sem("moe_done")
        gate_ready = sem("gate_ready")
        sig_ready = sem("sig_ready")
        h_ready = sem("h_ready")
        h_t_ready = sem("h_t_ready")
        h_t_read = sem("h_t_read")
        y_read = sem("y_read")
        spread = sem("spread")
        spread_read = sem("spread_read")
        final_scaled = sem("final_scaled")
        final_ready = [sem(f"final_ready{t}") for t in range(NTILE)]

        block = ctx.enter_context(nc.Block())

        def reg(engine, value, top):
            return value if isinstance(value, int) else engine.snap(value, min_val=0, max_val=top)

        def tokens_most(engine):
            return engine.value_load(most_i[0:1, 0:1], min_val=0, max_val=T)

        def rounds_after_first(engine, tokens, run):
            with engine.If(tokens > SLOTS):
                with engine.Fori(1, ROUNDS) as r:
                    with engine.If(tokens > r * SLOTS):
                        run(r)
                    engine.nop()
                engine.nop()
            engine.nop()

        @block.sync
        def _(sp):
            nc.sync.dma_start(x_acc[:, 0, :], x_prompt[0][0:P, :]).then_inc(x_landed[0], 16)
            nc.sync.dma_start(x_acc[:, 1, :], x_prompt[0][P:2 * P, :]).then_inc(x_landed[1], 16)
            nc.sync.dma_start(x_acc[0:NS, 2, :], x_sample.rearrange("b t d -> (b t) d")).then_inc(x_landed[2], 16)
            for src, at_row in ((conv_w[0].rearrange("w (k c) -> (w k) c", c=P), CONV_W),
                                (pool_scale[0].rearrange("(k c) -> k c", c=P), SCALE),
                                (norm_ffn_g[0].rearrange("(k c) -> k c", c=P), G_FFN)):
                nc.sync.dma_start(vec_rows[at_row:at_row + src.shape[0], :], src).then_inc(vecs_landed, 16)
            nc.sync.dma_start(conv_rows, state_conv[0].rearrange("b j c -> (b j) c")).then_inc(states_landed, 16)
            nc.sync.dma_start(pool_rows, state_pool[0].rearrange("b j c -> (b j) c")).then_inc(states_landed, 16)
            for j, col in enumerate((1, 2, 3, 0)):
                nc.sync.dma_start(w_in_sb[:, j], w_in[0][:, col * DC:(col + 1) * DC].rearrange(
                    "(k p) n -> p k n", p=P)).then_inc(w_in_landed[j], 16)
            nc.sync.dma_start(router_f[:], router_w[0].rearrange("(k p) e -> p k e", p=P)).then_inc(consts_landed, 16)
            nc.sync.dma_start(bias_e[:], router_b.to_broadcast([P, E])).then_inc(consts_landed, 16)
            nc.sync.dma_start(pool_f[:], pool_w[0].rearrange("g c d -> c g d")).then_inc(consts_landed, 16)
            nc.sync.dma_start(gain[:], norm_ffn_g.to_broadcast([P, D])).then_inc(consts_landed, 16)
            for c in range(W1N):
                nc.sync.dma_start(b1_rows[c * E:(c + 1) * E, :], exp_b1[0][:, c * BANK:(c + 1) * BANK]).then_inc(consts_landed, 16)
            for c in range(YN):
                nc.sync.dma_start(b2_rows[c * E:(c + 1) * E, :], exp_b2[0][:, c * BANK:(c + 1) * BANK]).then_inc(consts_landed, 16)
            nc.sync.dma_start(w_out_sb, w_out[0].rearrange("(k p) n -> p k n", p=P)).then_inc(w_out_landed, 16)

            def load_w1(pair, k, n):
                if n is not None:
                    sp.wait_ge(w1_used, n * KD + k - 3)
                nc.sync.dma_start(w1_ring[:, k % 4], exp_w1[0][bass.ds(pair * 2, 2), k * P:(k + 1) * P, :]
                                  .rearrange("e p n -> p e n")).then_inc(w1_landed[k % 4], 16)

            def load_w2(pair, s):
                for e in range(2):
                    nc.sync.dma_start(w2_ring[:, s, e], exp_w2[0][bass.ds(pair * 2 + e, 1), s * 2 * P:(s + 1) * 2 * P, :]
                                      .rearrange("e (k p) n -> p (e k) n", p=P)).then_inc(w2_landed[s], 16)

            def load_w1_half(r, pair, first):
                n = reg(nc.sync, r * PAIRS + pair, ROUNDS * PAIRS)
                for k in range(first, first + 4):
                    load_w1(pair, k, n)

            def load_w2_slots(r, pair, slots):
                n = reg(nc.sync, r * PAIRS + pair, ROUNDS * PAIRS)
                for s in slots:
                    sp.wait_ge(w2_used, n * 4 + s - 3)
                    load_w2(pair, s)

            def step(r, pair, early=0):
                load_w2_slots(r, pair - 1, range(early))
                load_w1_half(r, pair, 0)
                load_w2_slots(r, pair - 1, range(early, 4))
                load_w1_half(r, pair, 4)

            def pairs(r):
                if isinstance(r, int):
                    load_w1_half(r, 1, 0)
                    load_w1_half(r, 1, 4)
                    for i, early in enumerate(W2_EARLY):
                        step(r, 2 + i, early)
                    first = 2 + len(W2_EARLY)
                else:
                    load_w1_half(r, 0, 0)
                    load_w1_half(r, 0, 4)
                    first = 1
                with nc.sync.Fori(first, PAIRS) as pair:
                    step(r, pair)
                load_w2_slots(r, PAIRS - 1, range(4))

            for k in range(4):
                sp.wait_ge(w_in_used, KD * (k + 1))
                load_w1(0, k, None)
            sp.wait_ge(z_ready, 2)
            load_w2(0, 2)
            load_w2(0, 3)
            for i, s in enumerate((1, 0)):
                sp.wait_ge(w_out_used, i + 1)
                load_w2(0, s)
            load_w1_half(0, 0, 4)
            pairs(0)
            sp.wait_ge(counts_ready, 1)
            rounds_after_first(nc.sync, tokens_most(nc.sync), pairs)

            for t in range(NTILE):
                sp.wait_ge(final_ready[t], 1)
                dst = y_prompt[0][t * P:(t + 1) * P, :] if t < 2 else y_sample.rearrange("b t d -> (b t) d")
                nc.sync.dma_start(dst, x_norm[0:rows[t], t, :]).then_inc(stored, 16)
            sp.wait_ge(stored, 16 * (NTILE + 1))
            sp.wait_ge(cache_stored, 16 * (3 + NB))

        @block.tensor
        def _(pe):
            mm = nc.tensor.matmul

            pe.wait_ge(consts_made, 1)
            pe.wait_ge(vecs_landed, 16 * 4)
            nc.tensor.transpose(psum[:, 0, 0:4 * KD], vec_rows[:], ident[0:4 * KD, 0:4 * KD]).then_inc(front_t, 1)

            pe.wait_ge(scaled, NTILE)
            pe.wait_ge(front_t_read, 1)
            for k in range(KD):
                for t in range(NTILE):
                    last = nc.tensor.transpose(psum[:, k, t * P:t * P + rows[t]],
                                               x_norm[0:rows[t], t, k * P:(k + 1) * P],
                                               ident[0:rows[t], 0:rows[t]])
                last.then_inc(x_t_ready, 1)

            for j in range(4):
                if j == 1:
                    pe.wait_ge(states_landed, 16 * 2)
                    for i in range(KC):
                        last = nc.tensor.transpose(psum[:, 4, 16 * i:16 * i + NB * CB], conv_rows[:, i * P:(i + 1) * P],
                                                   ident[0:NB * CB, 0:NB * CB])
                    last.then_inc(front_t, 1)
                    for i in range(NG):
                        last = nc.tensor.transpose(psum[:, 5, P * i:P * i + NB * PB], pool_rows[:, i * P:(i + 1) * P],
                                                   ident[0:NB * PB, 0:NB * PB])
                    last.then_inc(front_t, 1)
                    pe.wait_ge(front_t_read, 3)
                if j >= 2:
                    pe.wait_ge(proj_read, j - 1)
                for k in range(KD):
                    if j == 0 and k == 0:
                        pe.wait_ge(x_low_ready, 4)
                    elif j == 0 and k >= 4:
                        pe.wait_ge(x_low_ready, k + 1)
                    if j == 3 and k == 2:
                        pe.wait_ge(last_ready, 1)
                        for i in range(KC):
                            nc.tensor.transpose(psum[0:CB, 0, i * P:(i + 1) * P], u_pad[:, i, NP:NP + CB], ident[:])
                            nc.tensor.transpose(psum[0:NB * CB, 1, i * P:(i + 1) * P], u_last[:, i, :], ident[:])
                            nc.tensor.transpose(psum[0:PB, 2, i * P:(i + 1) * P], v_pad[:, i, NP:NP + PB], ident[:])
                            last = nc.tensor.transpose(psum[0:NS, 3, i * P:(i + 1) * P], v_last[:, i, :], ident[:])
                        last.then_inc(cache_ready, 1)
                    if j == 3 and k == 6:
                        pe.wait_ge(pooled, 1)
                        pe.wait_ge(cache_read, 1)
                        pe.wait_ge(consts_landed, 16 * 10)
                        for g in range(NG):
                            last = mm(psum[:, g, 0:T], pool_f[:, g, :], p_t[:, g, :], start=True, stop=True)
                        last.then_inc(z_pool_ready, 1)
                    pe.wait_ge(w_low_ready, KD * j + k + 1)
                    for m in range(KC):
                        cols = slice(m * P, (m + 1) * P)
                        w_h, w_l = w_high[:, (KD * j + k) % 3, cols], w_low[:, j, k, cols]
                        x_h, x_l = x_parts[:, 0, k, :], x_parts[:, 1, k, :]
                        out = psum[:, 4 * (j % 2) + m, 0:T]
                        mm(out, w_h, x_h, start=(k == 0), stop=False)
                        mm(out, w_h, x_l, start=False, stop=False)
                        last = mm(out, w_l, x_h, start=False, stop=(k == KD - 1))
                    last.then_inc(w_in_used, 1)

            pe.wait_ge(w_out_landed, 16)
            for half_k in (1, 0):
                for t in MIX_ORDER:
                    if half_k and t == MIX_ORDER[0]:
                        pe.wait_ge(z_pool_scaled, 1)
                    elif half_k and t == MIX_ORDER[2]:
                        pe.wait_ge(z_ready, 2)
                    for n in range(YN):
                        for q in range(4):
                            k = 4 * half_k + q
                            z = (z_pool if half_k else z_conv)[:, q, t * P:t * P + rows[t]]
                            if t == 2:
                                last = mm(psum[q * NS:(q + 1) * NS, mix_bank(t, n), :], z,
                                          w_out_sb[:, k, n * BANK:(n + 1) * BANK],
                                          start=(half_k == 1), stop=(half_k == 0))
                            else:
                                last = mm(psum[:, mix_bank(t, n), :], z,
                                          w_out_sb[:, k, n * BANK:(n + 1) * BANK], start=(k == 4), stop=(k == 3))
                        if not half_k and (t, n) != (1, YN - 1):
                            last.then_inc(mixed, 1)
                last.then_inc(w_out_used, 1)

            for k in range(KD):
                for t in range(NTILE):
                    if k == 0:
                        pe.wait_ge(residual, YN * NTILE)
                    last = nc.tensor.transpose(psum[:, k, t * P:t * P + rows[t]],
                                               x_acc[0:rows[t], t, k * P:(k + 1) * P],
                                               ident[0:rows[t], 0:rows[t]])
                last.then_inc(x_t_ready, 1)
            for k in range(KD):
                pe.wait_ge(x_t_act if k % 2 else x_t_dve, k // 2 + 1)
                last = mm(psum[(k % 4) * E:(k % 4 + 1) * E, 0, 0:T], router_g[:, k, :], x_t[:, k, :],
                          start=(k < 4), stop=(k >= 4))
            last.then_inc(logit_parts_ready, 1)
            pe.wait_ge(logit_parts_read, 1)
            for t in range(NTILE):
                last = mm(psum[0:rows[t], 1, t * E:(t + 1) * E], logit_parts[:, t * P:t * P + rows[t]],
                          pick_table[:, 0:E], start=True, stop=True)
            last.then_inc(logits_ready, 1)

            def add_b1(blocks):
                for c in blocks:
                    last = mm(psum[:, c, :], pick_b1[c * E:(c + 1) * E], b1_rows[c * E:(c + 1) * E, :],
                              start=True, stop=False, skip_group_check=True)
                return last

            pe.wait_ge(picked_b1, 1)
            add_b1((0, 2, 3))
            pe.wait_ge(mask_ready, 1)
            mm(psum[:, 7, 0:(NTILE + 1) * E], before[:], mask[:], start=True, stop=False)
            for t in range(1, NTILE + 1):
                last = mm(psum[:, 7, t * E:(NTILE + 1) * E], ones[:], mask[:, 0:NTILE + 1 - t, :],
                          start=False, stop=(t == NTILE))
            last.then_inc(ranks_ready, 1)
            add_b1((1,))

            def gather(blocks):
                for k in blocks:
                    for t in range(NTILE):
                        last = mm(psum[:, 4 + k // 4, (k % 4) * P:(k % 4 + 1) * P],
                                  x_norm[0:rows[t], t, k * P:(k + 1) * P], place[0:rows[t], t],
                                  start=(t == 0), stop=(t == NTILE - 1))
                    if k % 4 == 3:
                        last.then_inc(gathered, 1)

            def turn_back():
                for t in range(NTILE):
                    last = nc.tensor.transpose(psum[:, 6, t * P:t * P + rows[t]], gated[0:rows[t], t],
                                               ident[0:rows[t], 0:rows[t]])
                last.then_inc(back_ready, 1)

            def first_product(n, first):
                pe.wait_ge(gathered_read, 2 * n + first // 4 + 1)
                for k in range(first, first + 4):
                    pe.wait_ge(w1_landed[k % 4], 32 * n + 16 * (k // 4) + 16)
                    for c in range(W1N):
                        for e in range(2):
                            last = mm(psum[e * SLOTS:(e + 1) * SLOTS, c, :], gathered_t[:, k, e, :],
                                      w1_ring[:, k % 4, e, c * BANK:(c + 1) * BANK],
                                      start=False, stop=(k == KD - 1), skip_group_check=True)
                    last.then_inc(w1_used, 1)

            def pair_steps(n, final):
                first_product(n, 4)
                if not final:
                    pe.wait_ge(slots_ready, n + 2)
                    pe.wait_ge(y_read, 2 * n + 2)
                    gather(range(KD))
                pe.wait_ge(back_read, n + 1)
                pe.wait_ge(spread_read, 6 * n + 6)

                def transpose_h(half_h):
                    pe.wait_ge(h_ready, 2 * n + half_h + 1)
                    for k in range(4):
                        last = nc.tensor.transpose(psum[:, 6 + half_h, k * P:(k + 1) * P],
                                                   hidden[:, 0, half_h, k * P:(k + 1) * P], ident[:])
                    last.then_inc(h_t_ready, 1)

                def add_b2():
                    pe.wait_ge(picked_b2, n + 1)
                    for c in range(YN):
                        mm(psum[:, 4 + c, :], pick_b2[c * E:(c + 1) * E], b2_rows[c * E:(c + 1) * E, :],
                           start=True, stop=False, skip_group_check=True)

                if final:
                    pe.wait_ge(y_read, 2 * n + 2)
                    add_b2()
                    transpose_h(0)
                else:
                    transpose_h(0)
                    transpose_h(1)
                    pe.wait_ge(picked_b1, n + 2)
                    add_b1(range(W1N))
                    first_product(n + 1, 0)
                    pe.wait_ge(gathered_read, 2 * n + 4)
                    add_b2()
                for s in range(4):
                    if final and s == 2:
                        transpose_h(1)
                    if s % 2 == 0:
                        pe.wait_ge(h_t_read, 2 * n + s // 2 + 1)
                    pe.wait_ge(w2_landed[s], 32 * n + 32)
                    for c in range(YN):
                        for k in (2 * s, 2 * s + 1):
                            for e in range(2):
                                last = mm(psum[e * SLOTS:(e + 1) * SLOTS, 4 + c, :], h_t[:, k, e, :],
                                          w2_ring[:, s, e, k % 2, c * BANK:(c + 1) * BANK],
                                          start=False, stop=(k == KD - 1), skip_group_check=True)
                        if s == 3 and c < YN - 1:
                            last.then_inc(y_part, 1)
                    last.then_inc(w2_used, 1)
                for j in range(YN * NTILE):
                    c, t = divmod(j, NTILE)
                    if t == 0:
                        pe.wait_ge(y_read, 2 * n + 3 + c)
                    if j < 2:
                        pe.wait_ge(h_t_read, 2 * n + 2)
                    else:
                        pe.wait_ge(spread_read, 6 * n + 5 + j)
                    last = mm(psum[0:rows[t], 6 + j % 2, :], back[:, t * P:t * P + rows[t]],
                              y_slots[:, c, :], start=True, stop=True)
                    last.then_inc(spread, 1)
                if not final:
                    pe.wait_ge(spread_read, 6 * n + 11)
                    turn_back()

            def round_of(r):
                n0 = reg(nc.tensor, r * PAIRS, ROUNDS * PAIRS)
                if isinstance(r, int):
                    pe.wait_ge(x_norm_ready, 1)
                else:
                    pe.wait_ge(y_read, 2 * n0 + 2)
                    pe.wait_ge(spread_read, 6 * n0 + 6)
                    pe.wait_ge(picked_b1, n0 + 1)
                    add_b1(range(W1N))
                pe.wait_ge(slots_ready, n0 + 1)
                gather(range(4))
                first_product(n0, 0)
                gather(range(4, KD))
                turn_back()
                with nc.tensor.Fori(0, PAIRS - 1) as pair:
                    pair_steps(reg(nc.tensor, r * PAIRS + pair, ROUNDS * PAIRS), False)
                pair_steps(reg(nc.tensor, r * PAIRS + PAIRS - 1, ROUNDS * PAIRS), True)

            round_of(0)
            pe.wait_ge(counts_ready, 1)
            rounds_after_first(nc.tensor, tokens_most(nc.tensor), round_of)

        @block.scalar
        def _(act):
            A = nc.scalar.activation

            nc.scalar.dma_start(vec_rows[G_MIX:G_MIX + KD, :],
                                norm_mix_g[0].rearrange("(k c) -> k c", c=P)).then_inc(vecs_landed, 16)
            act.wait_ge(presets_made, 1)
            A(warm[:], half[:, 0:1], ACT.Square)
            for t in range(NTILE):
                if t == 1:
                    continue
                act.wait_ge(x_landed[t], 16)
                A(x_norm[0:rows[t], t, :], x_acc[0:rows[t], t, :], ACT.Square,
                  accum_out=sumsq[0:rows[t], 0, t:t + 1]).then_inc(squares, 1)
            act.wait_ge(rms_ready, 1)
            act.wait_ge(squares, NTILE)
            A(x_norm[:, 1, :], x_acc[:, 1, :], ACT.Copy, scale=rms[:, 0, 1:2]).then_inc(scaled, 1)
            act.wait_ge(front_t_read, 1)
            def x_high(first, end):
                for k in range(first, end):
                    act.wait_ge(x_t_ready, k + 1)
                    A(x_parts[:, 0, k, :], psum[:, k, 0:T], ACT.Copy,
                      scale=vecs[:, G_MIX + k:G_MIX + k + 1]).then_inc(x_high_ready, 1)

            def high_parts(first, end):
                for c in range(first, end):
                    if c % KD == 0:
                        act.wait_ge(w_in_landed[c // KD], 16)
                    if c >= 3:
                        act.wait_ge(w_in_used, c - 2)
                    A(w_high[:, c % 3, :], w_in_sb[:, c // KD, c % KD, :], ACT.Copy).then_inc(w_high_ready, 1)

            x_high(0, 6)
            high_parts(0, 1)
            x_high(6, KD)
            high_parts(1, 3)
            nc.scalar.dma_start(new_pool_sample[0][:, 0:PB - NT, :], state_pool[0][:, NT:PB, :]).then_inc(stored, 16)
            high_parts(3, KD + 2)
            act.wait_ge(w_in_used, KD)
            A(c_gate, psum[:, 0:4, 0:T], ACT.Copy).then_inc(proj_read, 1)
            high_parts(KD + 2, 3 * KD + 2)
            act.wait_ge(w_in_used, 3 * KD)
            act.wait_ge(front_t_read, 5)
            A(v_pad[:, :, PB:PB + NP], psum[:, 0:4, 0:NP], ACT.Copy)
            for j in range(NG):
                last = A(v_pad[:, j, PS:PL].rearrange("p (b t) -> p b t", b=NB)[:, :, PB:PB + NT],
                         psum[:, j, NP:T].rearrange("p (b t) -> p b t", b=NB), ACT.Copy)
            last.then_inc(v_ready, 1)
            high_parts(3 * KD + 2, 3 * KD + 5)
            act.wait_ge(cache_ready, 1)
            A(cache_rows[0:CB, 0, :], psum[0:CB, 0, :], ACT.Copy)
            A(cache_rows[0:NB * CB, 1, :], psum[0:NB * CB, 1, :], ACT.Copy)
            A(cache_rows[0:PB, 2, :], psum[0:PB, 2, :], ACT.Copy)
            A(cache_rows_v[:], psum[0:NS, 3, :], ACT.Copy).then_inc(cache_read, 1)
            high_parts(3 * KD + 5, 4 * KD)
            act.wait_ge(z_pool_ready, 1)
            for g in range(NG):
                last = A(z_pool[:, g, :], psum[:, g, 0:T], ACT.Copy, scale=vecs[:, SCALE + g:SCALE + g + 1])
            last.then_inc(z_pool_scaled, 1)
            act.wait_ge(z_pool_scaled, 1)
            nc.scalar.sem_inc(z_ready, 1)
            act.wait_ge(cache_read, 1)
            nc.scalar.dma_start(new_conv_prompt[0, 0], cache_rows[0:CB, 0, :]).then_inc(cache_stored, 16)
            nc.scalar.dma_start(new_conv_sample[0].rearrange("b j c -> (b j) c"),
                                cache_rows[0:NB * CB, 1, :]).then_inc(cache_stored, 16)
            nc.scalar.dma_start(new_pool_prompt[0, 0], cache_rows[0:PB, 2, :]).then_inc(cache_stored, 16)
            for b in range(NB):
                nc.scalar.dma_start(new_pool_sample[0, b, PB - NT:PB, :],
                                    cache_rows_v[b * NT:(b + 1) * NT, :]).then_inc(cache_stored, 16)
            act.wait_ge(cache_stored, 16 * (3 + NB))
            for i, t in enumerate(MIX_ORDER):
                act.wait_ge(residual, YN * (i + 1))
                A(x_norm[0:rows[t], t, :], x_acc[0:rows[t], t, :], ACT.Square,
                  accum_out=sumsq[0:rows[t], 1, t:t + 1]).then_inc(squares, 1)
            for k in range(1, KD, 2):
                act.wait_ge(x_t_ready, KD + k + 1)
                A(x_t[:, k, :], psum[:, k, 0:T], ACT.Copy).then_inc(x_t_act, 1)
            act.wait_ge(logit_parts_ready, 1)
            A(logit_parts, psum[:, 0, 0:T], ACT.Copy).then_inc(logit_parts_read, 1)
            act.wait_ge(shifted_ready, 1)
            A(shifted[:], shifted[:], ACT.Exp).then_inc(exp_ready, 1)
            nc.scalar.sem_inc(y_read, 2)
            act.wait_ge(x_norm_ready, 1)
            nc.scalar.dma_start(gain[:], final_norm_g[None, :].to_broadcast([P, D])).then_inc(g_final_landed, 16)

            def copy_gathered(n):
                for b in range(2):
                    act.wait_ge(gathered, 2 * n + b + 1)
                    A(routed[:, 0, b * BANK:(b + 1) * BANK], psum[:, 4 + b, :], ACT.Copy).then_inc(gathered_read, 1)

            def copy_back(n):
                act.wait_ge(back_ready, n + 1)
                A(back[:], psum[:, 6, 0:T], ACT.Copy).then_inc(back_read, 1)

            def pair_steps(n, final):
                for b in range(2):
                    act.wait_ge(gate_ready, 2 * n + b + 1)
                    A(hidden[:, 2, b, :], hidden[:, 0, b, :], ACT.Sigmoid, scale=SWIGLU_ALPHA).then_inc(sig_ready, 1)
                if not final:
                    copy_gathered(n + 1)
                for b in range(2):
                    act.wait_ge(h_t_ready, 2 * n + b + 1)
                    A(routed[:, 1, b * BANK:(b + 1) * BANK], psum[:, 6 + b, :], ACT.Copy).then_inc(h_t_read, 1)
                for c in range(YN):
                    if c < YN - 1:
                        act.wait_ge(y_part, (YN - 1) * n + c + 1)
                    else:
                        act.wait_ge(w2_used, 4 * n + 4)
                    A(y_slots[:, c, :], psum[:, 4 + c, :], ACT.Copy).then_inc(y_read, 1)
                if not final:
                    copy_back(n + 1)

            def round_of(r):
                n0 = reg(nc.scalar, r * PAIRS, ROUNDS * PAIRS)
                copy_gathered(n0)
                copy_back(n0)
                with nc.scalar.Fori(0, PAIRS - 1) as pair:
                    pair_steps(reg(nc.scalar, r * PAIRS + pair, ROUNDS * PAIRS), False)
                pair_steps(reg(nc.scalar, r * PAIRS + PAIRS - 1, ROUNDS * PAIRS), True)

            round_of(0)
            act.wait_ge(counts_ready, 1)
            rounds_after_first(nc.scalar, tokens_most(nc.scalar), round_of)

            act.wait_ge(moe_done, 1)
            for t in (0, 2):
                A(x_norm[0:rows[t], t, :], x_acc[0:rows[t], t, :], ACT.Square,
                  accum_out=sumsq[0:rows[t], 2, t:t + 1]).then_inc(squares, 1)
            act.wait_ge(rms_ready, 3)
            act.wait_ge(squares, 3 * NTILE)
            for t in (1, 2):
                A(x_norm[0:rows[t], t, :], x_acc[0:rows[t], t, :], ACT.Copy, scale=rms[0:rows[t], 2, t:t + 1]).then_inc(final_scaled, 1)

        @block.vector
        def _(dve):
            V = nc.vector
            step = Counter(dve_step)

            def then(ins):
                step.inc(ins)
                dve.wait_ge(dve_step, step.now())

            V.memset(sumsq[:], 1.0)
            V.memset(half[:], -0.5)
            V.memset(logits[:], 0.0)
            V.memset(rank[:], -1.0)
            V.memset(combine[:], 0.0)
            V.memset(mask[:, NTILE, :], 0.0)
            V.memset(pick_table[:], 0.0).then_inc(presets_made, 1)
            dve.wait_ge(presets_made, 1)
            def squares_of(i):
                V.tensor_tensor_reduce(out=x_norm[:, 1, :], in0=x_acc[:, 1, :], in1=x_acc[:, 1, :], scale=1.0,
                                       scalar=0.0, op0=ALU.mult, op1=ALU.add,
                                       accum_out=sumsq[:, i, 1:2]).then_inc(squares, 1)

            dve.wait_ge(x_landed[1], 16)
            squares_of(0)
            dve.wait_ge(front_t, 1)
            V.tensor_copy(vecs[:], psum[:, 0, 0:4 * KD]).then_inc(front_t_read, 1)
            dve.wait_ge(rms_ready, 1)
            for t in (0, 2):
                V.tensor_scalar(x_norm[0:rows[t], t, :], x_acc[0:rows[t], t, :], rms[0:rows[t], 0, t:t + 1],
                                None, ALU.mult).then_inc(scaled, 1)
            dve.wait_ge(front_t_read, 1)
            for k in range(KD):
                dve.wait_ge(x_high_ready, k + 1)
                V.scalar_tensor_tensor(out=x_parts[:, 1, k, :], in0=psum[:, k, 0:T],
                                       scalar=vecs[:, G_MIX + k:G_MIX + k + 1],
                                       in1=x_parts[:, 0, k, :].bitcast(F32), op0=ALU.mult,
                                       op1=ALU.subtract).then_inc(x_low_ready, 1)
            dve.wait_ge(front_t, 3)
            for j in range(KC):
                last = V.tensor_copy(u_pad[:, j, CS:CL].rearrange("p (b t) -> p b t", b=NB)[:, :, 0:CB],
                                     psum[:, 4, 16 * j:16 * j + NB * CB].rearrange("p (b t) -> p b t", b=NB))
            last.then_inc(front_t_read, 1)
            for j in range(NG):
                last = V.tensor_copy(v_pad[:, j, PS:PL].rearrange("p (b t) -> p b t", b=NB)[:, :, 0:PB],
                                     psum[:, 5, P * j:P * j + NB * PB].rearrange("p (b t) -> p b t", b=NB))
            last.then_inc(front_t_read, 1)
            V.memset(u_pad[:, :, 0:CB], 0.0).then_inc(front_t_read, 1)
            V.memset(v_pad[:, :, 0:PB], 0.0).then_inc(front_t_read, 1)
            dve.wait_ge(consts_made, 1)
            for c in range(W1N):
                last = V.tensor_copy(pick_table[c * E:(c + 1) * E, 0:E], ident[c * E:(c + 1) * E, c * E:(c + 1) * E])
            then(last)

            def picked(pair):
                return pick_table[:, bass.ds(pair * 2, 2)].unsqueeze(2).to_broadcast([P, 2, SLOTS])

            V.tensor_copy(pick_b1[:], picked(0)).then_inc(picked_b1, 1)
            dve.wait_ge(consts_made, 2)
            then(V.reciprocal(ramp[:], ramp[:]))
            for g, w in enumerate(WINDOWS):
                last = V.tensor_scalar(fix[:, g, :], ramp[:], float(w), 1.0, ALU.mult, ALU.max)
            dve.wait_ge(consts_landed, 16 * 10)
            for k in range(KD):
                last = V.tensor_scalar(router_g[:, k, :], router_f[:, k, :], vecs[:, G_FFN + k:G_FFN + k + 1], None,
                                       ALU.mult)
            then(last)

            dve.wait_ge(proj_read, 1)
            dve.wait_ge(w_in_used, 2 * KD)
            V.tensor_tensor(u_pad[:, :, CB:CB + NP], psum[:, 4:8, 0:NP], c_gate[:, :, 0:NP], ALU.mult)
            for j in range(KC):
                last = V.tensor_tensor(u_pad[:, j, CS:CL].rearrange("p (b t) -> p b t", b=NB)[:, :, CB:CB + NT],
                                       psum[:, 4 + j, NP:T].rearrange("p (b t) -> p b t", b=NB),
                                       c_gate[:, j, NP:T].rearrange("p (b t) -> p b t", b=NB), ALU.mult)
            last.then_inc(proj_read, 1)
            dve.wait_ge(proj_read, 2)
            for w in range(3):
                for j in range(KC):
                    wcol = vecs[:, CONV_W + KC * w + j:CONV_W + KC * w + j + 1]
                    src = u_pad[:, j, w:w + CY]
                    if w == 0:
                        last = V.tensor_scalar(conv_y[:, j, 0:CY], src, wcol, None, ALU.mult)
                    else:
                        last = V.scalar_tensor_tensor(out=conv_y[:, j, 0:CY], in0=src, scalar=wcol,
                                                      in1=conv_y[:, j, 0:CY], op0=ALU.mult, op1=ALU.add)
                then(last)
            dve.wait_ge(v_ready, 1)
            V.tensor_copy(u_last.rearrange("p k (b t) -> p k b t", b=NB),
                          u_pad[:, :, CS:CL].rearrange("p k (b t) -> p k b t", b=NB)[:, :, :, NT:NT + CB])
            V.tensor_copy(v_last.rearrange("p k (b t) -> p k b t", b=NB),
                          v_pad[:, :, PS:PL].rearrange("p k (b t) -> p k b t", b=NB)[:, :, :, PB:PB + NT]).then_inc(last_ready, 1)
            then(V.tensor_tensor(sum_a[:, :, 1:PL], v_pad[:, :, 1:PL], v_pad[:, :, 0:PL - 1], ALU.add))
            then(V.tensor_tensor(sum_b[:, 1:4, 3:PL], sum_a[:, 1:4, 3:PL], sum_a[:, 1:4, 1:PL - 2], ALU.add))
            then(V.tensor_tensor(sum_a[:, 2:4, 7:PL], sum_b[:, 2:4, 7:PL], sum_b[:, 2:4, 3:PL - 4], ALU.add))
            then(V.tensor_tensor(sum_b[:, 3, 15:PL], sum_a[:, 3, 15:PL], sum_a[:, 3, 7:PL - 8], ALU.add))
            sums = (sum_a, sum_b, sum_a, sum_b)
            for g in range(NG):
                last = V.tensor_tensor(sums[g][:, g, PB:PB + 16], sums[g][:, g, PB:PB + 16], fix[:, g, :], ALU.mult)
            then(last)
            for g, w in enumerate(WINDOWS):
                V.scalar_tensor_tensor(out=p_t[:, g, 0:NP], in0=sums[g][:, g, PB:PB + NP], scalar=1.0 / w,
                                       in1=v_pad[:, g, PB:PB + NP], op0=ALU.mult, op1=ALU.subtract)
                tail_s = sums[g][:, g, PS:PL].rearrange("p (b t) -> p b t", b=NB)[:, :, PB:PB + NT]
                tail_v = v_pad[:, g, PS:PL].rearrange("p (b t) -> p b t", b=NB)[:, :, PB:PB + NT]
                last = V.scalar_tensor_tensor(out=p_t[:, g, NP:T].rearrange("p (b t) -> p b t", b=NB), in0=tail_s,
                                              scalar=1.0 / w, in1=tail_v, op0=ALU.mult, op1=ALU.subtract)
            last.then_inc(pooled, 1)
            dve.wait_ge(w_in_used, 4 * KD)
            V.tensor_tensor(z_conv[:, :, 0:NP], psum[:, 4:8, 0:NP], conv_y[:, :, 0:NP], ALU.mult)
            for j in range(KC):
                last = V.tensor_tensor(z_conv[:, j, NP:T].rearrange("p (b t) -> p b t", b=NB),
                                       psum[:, 4 + j, NP:T].rearrange("p (b t) -> p b t", b=NB),
                                       conv_y[:, j, CS:CL].rearrange("p (b t) -> p b t", b=NB)[:, :, 0:NT], ALU.mult)
            last.then_inc(z_ready, 1)
            dve.wait_ge(w_out_landed, 16)
            for i, t in enumerate(MIX_ORDER):
                for n in range(YN):
                    if (t, n) == (1, YN - 1):
                        dve.wait_ge(w_out_used, 2)
                    else:
                        dve.wait_ge(mixed, YN * i + n + 1)
                    own = x_acc[0:rows[t], t, n * BANK:(n + 1) * BANK]
                    for q in range(4 if t == 2 else 1):
                        last = V.tensor_tensor(own, own, psum[q * NS:q * NS + rows[t], mix_bank(t, n), :], ALU.add)
                        if t == 2 and q < 3:
                            then(last)
                    last.then_inc(residual, 1)
            for k in range(0, KD, 2):
                dve.wait_ge(x_t_ready, KD + k + 1)
                V.tensor_copy(x_t[:, k, :], psum[:, k, 0:T]).then_inc(x_t_dve, 1)

            dve.wait_ge(rms_ready, 2)
            dve.wait_ge(residual, YN * NTILE)
            dve.wait_ge(consts_landed, 16 * 10)
            for t in range(NTILE):
                last = V.scalar_tensor_tensor(out=x_norm[0:rows[t], t, :], in0=x_acc[0:rows[t], t, :],
                                              scalar=rms[0:rows[t], 1, t:t + 1], in1=gain[0:rows[t], :],
                                              op0=ALU.mult, op1=ALU.mult)
            last.then_inc(x_norm_ready, 1)
            dve.wait_ge(logits_ready, 1)
            for t in range(NTILE):
                last = V.scalar_tensor_tensor(out=logits[0:rows[t], t, :], in0=psum[0:rows[t], 1, t * E:(t + 1) * E],
                                              scalar=rms[0:rows[t], 1, t:t + 1], in1=bias_e[0:rows[t], :],
                                              op0=ALU.mult, op1=ALU.add)
            then(last)
            for t in range(NTILE):
                last = V.max(top8[:, t, :], logits[:, t, :])
            then(last)
            V.tensor_tensor(shifted[:], logits[:], top8[:, :, 0:1].to_broadcast([P, NTILE, E]),
                            ALU.subtract).then_inc(shifted_ready, 1)
            for t in range(NTILE):
                last = V.max_index(top_at[:, t, :], top8[:, t, :], logits[:, t, :])
            then(last)
            then(V.tensor_copy(top_f[:], top_at[:]))
            dve.wait_ge(consts_made, 2)
            for t in range(NTILE):
                last = V.tensor_tensor(match[:, t], expert_id[:].unsqueeze(2).to_broadcast([P, E, TOP_K]),
                                       top_f[:, t, 0:TOP_K].unsqueeze(1).to_broadcast([P, E, TOP_K]), ALU.is_equal)
            then(last)
            then(V.tensor_reduce(mask[:, 0:NTILE, :], match[:], AX.X, ALU.max))
            V.memset(mask[32:64, 2, :], 0.0)
            V.memset(mask[64:128, 2, :], 0.0).then_inc(mask_ready, 1)
            dve.wait_ge(mask_ready, 1)
            dve.wait_ge(exp_ready, 1)
            then(V.tensor_tensor(combine[:, :, 0:E], shifted[:], mask[:, 0:NTILE, :], ALU.mult))
            then(V.tensor_reduce(denom[:], combine[:, :, 0:E], AX.X, ALU.add))
            V.memset(denom[32:64, 2:3], 1.0)
            then(V.memset(denom[64:128, 2:3], 1.0))
            then(V.reciprocal(denom[:], denom[:]))
            V.tensor_tensor(combine[:, :, 0:E], combine[:, :, 0:E], denom[:].unsqueeze(2).to_broadcast([P, NTILE, E]),
                            ALU.mult).then_inc(combine_ready, 1)
            dve.wait_ge(combine_ready, 1)
            dve.wait_ge(ranks_ready, 1)
            then(V.scalar_tensor_tensor(out=rank[:, :, 0:E],
                                        in0=psum[:, 7, 0:NTILE * E].rearrange("p (t e) -> p t e", t=NTILE),
                                        scalar=1.0, in1=mask[:, 0:NTILE, :], op0=ALU.add, op1=ALU.mult))
            then(V.tensor_scalar(rank[:, :, 0:E], rank[:, :, 0:E], -1.0, None, ALU.add))
            dve.sem_inc(spread_read, NTILE * YN)

            def build(pair, n):
                def own(table):
                    return table[:, :, bass.ds(pair * 2, 2)].unsqueeze(3).to_broadcast([P, NTILE, 2, SLOTS])

                ids = slot_id[:].unsqueeze(1).unsqueeze(1).to_broadcast([P, NTILE, 2, SLOTS])
                V.tensor_tensor(place[:], ids, own(rank), ALU.is_equal).then_inc(dve_build, 1)
                dve.wait_ge(dve_build, n + 1)
                V.tensor_tensor(gated[:], place[:], own(combine), ALU.mult).then_inc(slots_ready, 1)

            def pair_steps(pair, n, final):
                if not final:
                    dve.wait_ge(back_ready, n + 1)
                    nxt = reg(nc.vector, pair + 1, PAIRS)
                    V.tensor_copy(pick_b1[:], picked(nxt)).then_inc(picked_b1, 1)
                    build(nxt, n + 1)
                V.tensor_copy(pick_b2[:], picked(pair)).then_inc(picked_b2, 1)
                dve.wait_ge(w1_used, KD * n + KD)
                for b in range(2):
                    V.tensor_scalar(hidden[:, 0, b, :], psum[:, b, :], SWIGLU_LIMIT, None,
                                    ALU.min).then_inc(gate_ready, 1)
                for b in range(2):
                    V.tensor_scalar(hidden[:, 1, b, :], psum[:, 2 + b, :], SWIGLU_LIMIT, -SWIGLU_LIMIT,
                                    ALU.min, ALU.max).then_inc(lin_step, 1)
                    dve.wait_ge(gate_ready, 2 * n + b + 1)
                    dve.wait_ge(lin_step, 4 * n + 2 * b + 1)
                    V.scalar_tensor_tensor(out=hidden[:, 1, b, :], in0=hidden[:, 1, b, :], scalar=1.0,
                                           in1=hidden[:, 0, b, :], op0=ALU.add, op1=ALU.mult).then_inc(lin_step, 1)
                    dve.wait_ge(lin_step, 4 * n + 2 * b + 2)
                    dve.wait_ge(sig_ready, 2 * n + b + 1)
                    V.tensor_tensor(hidden[:, 0, b, :], hidden[:, 1, b, :], hidden[:, 2, b, :],
                                    ALU.mult).then_inc(h_ready, 1)
                for j in range(YN * NTILE):
                    c, t = divmod(j, NTILE)
                    dve.wait_ge(spread, 6 * n + j + 1)
                    V.tensor_tensor(x_acc[0:rows[t], t, c * BANK:(c + 1) * BANK],
                                    x_acc[0:rows[t], t, c * BANK:(c + 1) * BANK],
                                    psum[0:rows[t], 6 + j % 2, :], ALU.add).then_inc(spread_read, 1)

            def round_of(r):
                n0 = reg(nc.vector, r * PAIRS, ROUNDS * PAIRS)
                if not isinstance(r, int):
                    V.tensor_copy(pick_b1[:], picked(0)).then_inc(picked_b1, 1)
                    V.tensor_scalar(slot_id[:], slot_id[:], float(SLOTS), None, ALU.add).then_inc(slot_step, 1)
                    dve.wait_ge(slot_step, r)
                build(0, n0)
                if isinstance(r, int):
                    then(V.reduce_max(most[:], psum[:, 7, NTILE * E:(NTILE + 1) * E], AX.X))
                    V.tensor_copy(most_i[:], most[:]).then_inc(counts_ready, 1)
                with nc.vector.Fori(0, PAIRS - 1) as pair:
                    pair_steps(pair, reg(nc.vector, r * PAIRS + pair, ROUNDS * PAIRS), False)
                pair_steps(PAIRS - 1, reg(nc.vector, r * PAIRS + PAIRS - 1, ROUNDS * PAIRS), True)

            round_of(0)
            dve.wait_ge(counts_ready, 1)
            rounds_after_first(nc.vector, tokens_most(nc.vector), round_of)
            V.memset(most[:], 0.0).then_inc(moe_done, 1)
            dve.wait_ge(moe_done, 1)
            squares_of(2)

            dve.wait_ge(rms_ready, 3)
            dve.wait_ge(squares, 3 * NTILE)
            dve.wait_ge(g_final_landed, 16)
            V.scalar_tensor_tensor(out=x_norm[:, 0, :], in0=x_acc[:, 0, :], scalar=rms[:, 2, 0:1], in1=gain[:],
                                   op0=ALU.mult, op1=ALU.mult).then_inc(final_ready[0], 1)
            dve.wait_ge(final_scaled, 1)
            V.tensor_tensor(x_norm[:, 1, :], x_norm[:, 1, :], gain[:], ALU.mult).then_inc(final_ready[1], 1)

        @block.gpsimd
        def _(pool):
            G = nc.gpsimd
            G.memset(ident[:], 0.0)
            G.memset(ones[:], 1.0).then_inc(pool_step, 1)
            pool.wait_ge(pool_step, 1)
            G.affine_select(out=ident[:], in_=ident[:], compare_op=ALU.not_equal, fill=1.0, base=0,
                            pattern=[[-1, P]], channel_multiplier=1).then_inc(consts_made, 1)
            G.affine_select(out=before[:], in_=ones[:], compare_op=ALU.is_ge, fill=0.0, base=-1,
                            pattern=[[1, P]], channel_multiplier=-1)
            G.iota(slot_id[:], pattern=[[1, SLOTS]], base=0, channel_multiplier=0, allow_small_or_imprecise_dtypes=True)
            G.iota(expert_id[:], pattern=[[1, E]], base=0, channel_multiplier=0, allow_small_or_imprecise_dtypes=True)
            G.iota(ramp[:], pattern=[[1, 16]], base=1, channel_multiplier=0,
                   allow_small_or_imprecise_dtypes=True).then_inc(consts_made, 1)
            pool.wait_ge(presets_made, 1)
            for i in range(3):
                if i == 2:
                    pool.wait_ge(moe_done, 1)
                pool.wait_ge(squares, NTILE * (i + 1))
                G.tensor_scalar(rms[:, i, :], sumsq[:, i, :], 1.0 / D, EPS, ALU.mult, ALU.add).then_inc(pool_step, 1)
                pool.wait_ge(pool_step, 2 + i)
                G.tensor_tensor(rms[:, i, :], rms[:, i, :], half[:], ALU.pow).then_inc(rms_ready, 1)
                if i == 0:
                    for c in range(4 * KD):
                        pool.wait_ge(w_high_ready, c + 1)
                        G.tensor_tensor(w_low[:, c // KD, c % KD, :], w_in_sb[:, c // KD, c % KD, :],
                                        w_high[:, c % 3, :].bitcast(F32), ALU.subtract).then_inc(w_low_ready, 1)
            pool.wait_ge(g_final_landed, 16)
            pool.wait_ge(final_scaled, 2)
            G.tensor_tensor(x_norm[0:NS, 2, :], x_norm[0:NS, 2, :], gain[0:NS, :], ALU.mult).then_inc(final_ready[2], 1)


INPUTS = ["x_prompt", "x_sample", "state_conv", "state_pool", "norm_mix_g", "w_in", "conv_w", "pool_w",
          "pool_scale", "w_out", "norm_ffn_g", "router_w", "router_b", "exp_w1", "exp_b1", "exp_w2",
          "exp_b2", "final_norm_g"]


def kernel(**inputs):
    import numpy as np
    import concourse.bacc as bacc
    from concourse.bass_utils import run_bass_kernel_spmd

    nc = bacc.Bacc("TRN2", target_bir_lowering=False, num_devices=1)
    arrays, aps = {}, []
    for name in INPUTS:
        a = np.ascontiguousarray(inputs[name])
        arrays[f"in_{name}"] = a
        aps.append(nc.dram_tensor(f"in_{name}", a.shape, mybir.dt.from_np(a.dtype), kind="ExternalInput").ap())
    xp, xs, sc, sp = (inputs[n].shape for n in ("x_prompt", "x_sample", "state_conv", "state_pool"))
    shapes = [xp, xs, (sc[0], xp[0]) + tuple(sc[2:]), (sp[0], xp[0]) + tuple(sp[2:]), sc, sp]
    for i, shape in enumerate(shapes):
        aps.append(nc.dram_tensor(f"out_{i}", tuple(shape), F32, kind="ExternalOutput").ap())
    hybrid_moe_layer(nc, *aps)
    results = run_bass_kernel_spmd(nc, [arrays], core_ids=[0]).results[0]
    return tuple(results[f"out_{i}"] for i in range(len(shapes)))
```

```python
from contextlib import ExitStack

import concourse.bass as bass
from concourse import mybir

F32 = mybir.dt.float32
F32R = mybir.dt.float32r
I32 = mybir.dt.int32
U32 = mybir.dt.uint32
ALU = mybir.AluOpType
ACT = mybir.ActivationFunctionType
AX = mybir.AxisListType

P = 128
BANK = 512
SWIGLU_LIMIT = 7.0
SWIGLU_ALPHA = 1.702
EPS = 1e-5
TOP_K = 4
WINDOWS = (2, 4, 8, 16)
SLOTS = 64
W2_EARLY = (4, 3, 2, 1)


class Counter:

    def __init__(self, sem):
        self.sem, self.base, self.n = sem, 0, 0

    def inc(self, instruction, by=1):
        instruction.then_inc(self.sem, by)
        self.n += by

    def now(self):
        return self.base + self.n


def hybrid_moe_layer(nc, x_prompt, x_sample, state_conv, state_pool, norm_mix_g, w_in, conv_w,
                     pool_w, pool_scale, w_out, norm_ffn_g, router_w, router_b, exp_w1, exp_b1,
                     exp_w2, exp_b2, final_norm_g, y_prompt, y_sample, new_conv_prompt,
                     new_pool_prompt, new_conv_sample, new_pool_sample):
    _, NP, D = x_prompt.shape
    NB, NT, _ = x_sample.shape
    NS = NB * NT
    T = NP + NS
    DC, DPL = state_conv.shape[3], state_pool.shape[3]
    CB, PB = state_conv.shape[2], state_pool.shape[2]
    E = router_w.shape[2]
    F = exp_w2.shape[2]
    KD = D // P
    KC = DC // P
    NTILE = (T + P - 1) // P
    rows = [min(P, T - P * t) for t in range(NTILE)]
    NG = len(WINDOWS)
    PAIRS = E // 2
    ROUNDS = (T + SLOTS - 1) // SLOTS
    W1N = 2 * F // BANK
    YN = D // BANK
    assert NP == 2 * P and NS == 32 and D == F and DC == DPL and KC == NG and D % BANK == 0

    CL = CB + NP + NB * (CB + NT)
    PL = PB + NP + NB * (PB + NT)
    CS, PS = CB + NP, PB + NP
    CY = CL - CB

    ctx = ExitStack()
    with ctx:
        def sb(name, shape, dt=F32):
            return ctx.enter_context(nc.sbuf_tensor(name, shape, dt))

        def sem(name):
            return ctx.enter_context(nc.semaphore(name))

        w1_ring = sb("w1_ring", [P, 4, 2, 2 * F])
        w1_ring_at = nc.sbuf_base - 4 * 4 * 2 * 2 * F
        w2_ring = sb("w2_ring", [P, 4, 2, 2, D])
        w2_ring_at = nc.sbuf_base - 4 * 4 * 4 * D
        x_acc = sb("x_acc", [P, NTILE, D])
        x_norm = sb("x_norm", [P, NTILE, D])
        work = sb("work", [P, 2, 3 * D])
        work_at = nc.sbuf_base - 4 * 2 * 3 * D
        hidden = work[:, 0, :].rearrange("p (a b n) -> p a b n", a=3, b=2)
        routed = work[:, 1, :].rearrange("p (a n) -> p a n", a=3)
        b1_rows = sb("b1_rows", [W1N * E, BANK])
        b2_rows = sb("b2_rows", [YN * E, BANK])
        gain = sb("gain", [P, D])
        back = sb("back", [P, T])
        place = sb("place", [P, NTILE, 2, SLOTS])
        gated = sb("gated", [P, NTILE, 2, SLOTS])
        pick_b1 = sb("pick_b1", [P, 2, SLOTS])
        pick_b2 = sb("pick_b2", [P, 2, SLOTS])
        pick_table = sb("pick_table", [P, E + 2])
        ident = sb("ident", [P, P])
        before = sb("before", [P, P])
        ones = sb("ones", [P, P])
        slot_id = sb("slot_id", [P, SLOTS])
        expert_id = sb("expert_id", [P, E])
        vec_rows = sb("vec_rows", [4 * KD, P])
        vecs = sb("vecs", [P, 4 * KD])
        router_f = sb("router_f", [P, KD, E])
        router_g = sb("router_g", [P, KD, E])
        bias_e = sb("bias_e", [P, E])
        pool_f = sb("pool_f", [P, NG, P])
        fix = sb("fix", [P, NG, 16])
        ramp = sb("ramp", [P, 16])
        warm = sb("warm", [P, 1])
        sumsq = sb("sumsq", [P, 3, NTILE])
        sumsq_right = sb("sumsq_right", [P, NTILE])
        rms = sb("rms", [P, 3, NTILE])
        half = sb("half", [P, NTILE])
        logits = sb("logits", [P, NTILE, E])
        top8 = sb("top8", [P, NTILE, 8])
        top_at = sb("top_at", [P, NTILE, 8], U32)
        top_f = sb("top_f", [P, NTILE, 8])
        mask = sb("mask", [P, NTILE + 1, E])
        shifted = sb("shifted", [P, NTILE, E])
        combine = sb("combine", [P, NTILE, E + 2])
        rank = sb("rank", [P, NTILE, E + 2])
        denom = sb("denom", [P, NTILE])
        most = sb("most", [P, 1])
        most_i = sb("most_i", [P, 1], I32)
        psum = ctx.enter_context(nc.psum_tensor("psum", [P, 8, BANK], F32))

        w_in_sb = w1_ring[:].rearrange("p s e n -> p s (e n)").rearrange("p s (k n) -> p s k n", k=KD)
        w2_flat = w2_ring[:].rearrange("p s e k n -> p (s e k n)")
        w_out_sb = w2_flat[:, 0:KD * D].rearrange("p (k n) -> p k n", k=KD)
        at = KD * D

        def scratch(blocks, length):
            nonlocal at
            v = w2_flat[:, at:at + blocks * length].rearrange("p (k n) -> p k n", k=blocks)
            at += blocks * length
            return v

        u_pad = scratch(KC, CL)
        v_pad = scratch(NG, PL)
        sum_a = scratch(NG, PL)
        sum_b = scratch(NG, PL)
        conv_y = scratch(KC, CL)
        assert at <= 4 * 4 * D
        flat_h = work[:, 0, :]
        x_t = flat_h[:, 0:KD * T].rearrange("p (k n) -> p k n", k=KD)
        flat_r = work[:, 1, :]
        match = flat_h[:, KD * T:KD * T + NTILE * E * TOP_K].rearrange("p (t e k) -> p t e k", t=NTILE, k=TOP_K)
        logit_parts = flat_r[:, 0:T]
        flat_n = x_norm[:].rearrange("p a n -> p (a n)")
        c_gate = flat_n[:, 0:KC * T].rearrange("p (k n) -> p k n", k=KC)
        p_t = c_gate
        x_parts = nc.alloc_sbuf_tensor_at("x_parts", [P, 2, KD, T], F32R, offset=work_at)
        w_high = nc.alloc_sbuf_tensor_at("w_high", [P, 3, DC], F32R, offset=work_at + 4 * 2 * KD * T)
        assert 2 * KD * T + 3 * DC <= 2 * 3 * D
        w_low = nc.alloc_sbuf_tensor_at("w_low", [P, 4, KD, DC], F32R, offset=w1_ring_at)
        w_out_low = nc.alloc_sbuf_tensor_at("w_out_low", [P, KD, D], F32R, offset=w2_ring_at)
        z_pool_parts = nc.alloc_sbuf_tensor_at("z_pool_parts", [P, NG, 2 * T], F32R, offset=w2_ring_at + 4 * (KD * D + KC * CL))
        z_conv = flat_h[:, 0:KC * T].rearrange("p (k n) -> p k n", k=KC)
        z_conv_parts = nc.alloc_sbuf_tensor_at("z_conv_parts", [P, KC, 2 * T], F32R, offset=work_at + 4 * KC * T)
        HIGH, LOW_SAMPLE, LOW_PROMPT = slice(0, T), slice(T, T + NS), slice(T + NS, 2 * T)
        OUT_BLOCKS = [(k, n) for k in range(KC, KD) for n in range(YN)] + [(k, n) for n in range(YN) for k in range(KC)]
        IN_BLOCKS = 4 * KD
        conv_rows = sum_a[0:NB * CB].rearrange("p k n -> p (k n)")[:, 0:DC]
        pool_rows = sum_b[0:NB * PB].rearrange("p k n -> p (k n)")[:, 0:DPL]
        cache_at = KC * T
        cache_rows = flat_n[:, cache_at:cache_at + 3 * DC].rearrange("p (k n) -> p k n", k=3)
        cache_rows_v = sb("cache_rows_v", [NS, DPL])
        last_at = cache_at + 3 * DC
        u_last = flat_n[:, last_at:last_at + KC * NB * CB].rearrange("p (k n) -> p k n", k=KC)
        v_last = flat_n[:, last_at + KC * NB * CB:last_at + KC * (NB * CB + NS)].rearrange("p (k n) -> p k n", k=NG)
        gathered_t = routed[:, 0, :].rearrange("p (k e s) -> p k e s", k=KD, e=2)
        h_t = routed[:, 1, :].rearrange("p (k e s) -> p k e s", k=KD, e=2)
        y_slots = routed[:, 2, :].rearrange("p (n c) -> p n c", n=YN)

        MIX_ORDER = (2, 0, 1)

        def mix_bank(t, n):
            return YN * MIX_ORDER.index(t) + n

        NORM_SQUARES = (NTILE, 3 * NTILE, 4 * NTILE)

        G_MIX, CONV_W, SCALE, G_FFN = 0, KD, KD + 3 * KC, 2 * KD + 2 * KC
        assert G_FFN == 3 * KD

        x_landed = [sem(f"x_landed{t}") for t in range(NTILE)]
        w_in_landed = [sem(f"w_in_landed{j}") for j in range(4)]
        w_in_begun = sem("w_in_begun")
        w_out_landed = sem("w_out_landed")
        vecs_landed = sem("vecs_landed")
        states_landed = sem("states_landed")
        consts_landed = sem("consts_landed")
        w1_landed = [sem(f"w1_landed{s}") for s in range(4)]
        w2_landed = [sem(f"w2_landed{s}") for s in range(4)]
        g_final_landed = sem("g_final_landed")
        stored = sem("stored")
        dve_step = sem("dve_step")
        pool_step = sem("pool_step")
        consts_made = sem("consts_made")
        presets_made = sem("presets_made")
        v_ready = sem("v_ready")
        last_ready = sem("last_ready")
        cache_read = sem("cache_read")
        cache_stored = sem("cache_stored")
        squares = sem("squares")
        rms_ready = sem("rms_ready")
        scaled = sem("scaled")
        front_t = sem("front_t")
        front_t_read = sem("front_t_read")
        x_high_ready = sem("x_high_ready")
        x_low_ready = sem("x_low_ready")
        w_high_ready = sem("w_high_ready")
        w_low_ready = sem("w_low_ready")
        w_mix_used = sem("w_mix_used")
        x_t_ready = sem("x_t_ready")
        x_t_dve = sem("x_t_dve")
        x_t_act = sem("x_t_act")
        proj_read = sem("proj_read")
        pooled = sem("pooled")
        z_pool_ready = sem("z_pool_ready")
        z_pool_high_ready = sem("z_pool_high_ready")
        z_pool_low_ready = sem("z_pool_low_ready")
        z_conv_made = sem("z_conv_made")
        z_conv_high_ready = sem("z_conv_high_ready")
        z_conv_low_ready = sem("z_conv_low_ready")
        mixed = sem("mixed")
        residual = sem("residual")
        logit_parts_ready = sem("logit_parts_ready")
        logit_parts_read = sem("logit_parts_read")
        logits_ready = sem("logits_ready")
        cache_ready = sem("cache_ready")
        shifted_ready = sem("shifted_ready")
        exp_ready = sem("exp_ready")
        mask_ready = sem("mask_ready")
        ranks_ready = sem("ranks_ready")
        combine_ready = sem("combine_ready")
        x_norm_ready = sem("x_norm_ready")
        counts_ready = sem("counts_ready")
        w1_used = sem("w1_used")
        y_part = sem("y_part")
        w2_used = sem("w2_used")
        place_ready = sem("place_ready")
        gated_ready = sem("gated_ready")
        first_gathered = sem("first_gathered")
        first_copied = sem("first_copied")
        gathered = sem("gathered")
        gathered_read = sem("gathered_read")
        back_ready = sem("back_ready")
        back_read = sem("back_read")
        picked_b1 = sem("picked_b1")
        picked_b2 = sem("picked_b2")
        slot_step = sem("slot_step")
        lin_step = sem("lin_step")
        moe_done = sem("moe_done")
        gate_ready = sem("gate_ready")
        sig_ready = sem("sig_ready")
        h_ready = sem("h_ready")
        h_t_ready = sem("h_t_ready")
        h_t_read = sem("h_t_read")
        y_read = sem("y_read")
        spread = sem("spread")
        spread_read = sem("spread_read")
        final_scaled = sem("final_scaled")
        final_ready = [sem(f"final_ready{t}") for t in range(NTILE)]

        block = ctx.enter_context(nc.Block())

        def reg(engine, value, top):
            return value if isinstance(value, int) else engine.snap(value, min_val=0, max_val=top)

        def tokens_most(engine):
            return engine.value_load(most_i[0:1, 0:1], min_val=0, max_val=T)

        def rounds_after_first(engine, tokens, run):
            with engine.If(tokens > SLOTS):
                with engine.Fori(1, ROUNDS) as r:
                    with engine.If(tokens > r * SLOTS):
                        run(r)
                    engine.nop()
                engine.nop()
            engine.nop()

        @block.sync
        def _(sp):
            nc.sync.dma_start(x_acc[:, 0, :], x_prompt[0][0:P, :]).then_inc(x_landed[0], 16)
            nc.sync.dma_start(x_acc[:, 1, :], x_prompt[0][P:2 * P, :]).then_inc(x_landed[1], 16)
            nc.sync.dma_start(x_acc[0:NS, 2, :], x_sample.rearrange("b t d -> (b t) d")).then_inc(x_landed[2], 16)
            for src, at_row in ((conv_w[0].rearrange("w (k c) -> (w k) c", c=P), CONV_W),
                                (pool_scale[0].rearrange("(k c) -> k c", c=P), SCALE),
                                (norm_ffn_g[0].rearrange("(k c) -> k c", c=P), G_FFN)):
                nc.sync.dma_start(vec_rows[at_row:at_row + src.shape[0], :], src).then_inc(vecs_landed, 16)
            for j, col in enumerate((1, 2, 3, 0)):
                w_in_cols = w_in[0][:, col * DC:(col + 1) * DC].rearrange("(k p) n -> p k n", p=P)
                if j == 0:
                    nc.sync.dma_start(w_in_sb[:, j, 0:4], w_in_cols[:, 0:4]).then_inc(w_in_begun, 16)
                    nc.sync.dma_start(w_in_sb[:, j, 4:KD], w_in_cols[:, 4:KD]).then_inc(w_in_landed[j], 16)
                    nc.sync.dma_start(conv_rows, state_conv[0].rearrange("b j c -> (b j) c")).then_inc(states_landed, 16)
                    nc.sync.dma_start(pool_rows, state_pool[0].rearrange("b j c -> (b j) c")).then_inc(states_landed, 16)
                else:
                    nc.sync.dma_start(w_in_sb[:, j], w_in_cols).then_inc(w_in_landed[j], 16)
            nc.sync.dma_start(router_f[:], router_w[0].rearrange("(k p) e -> p k e", p=P)).then_inc(consts_landed, 16)
            nc.sync.dma_start(bias_e[:], router_b.to_broadcast([P, E])).then_inc(consts_landed, 16)
            nc.sync.dma_start(pool_f[:], pool_w[0].rearrange("g c d -> c g d")).then_inc(consts_landed, 16)
            nc.sync.dma_start(gain[:], norm_ffn_g.to_broadcast([P, D])).then_inc(consts_landed, 16)
            for c in range(W1N):
                nc.sync.dma_start(b1_rows[c * E:(c + 1) * E, :], exp_b1[0][:, c * BANK:(c + 1) * BANK]).then_inc(consts_landed, 16)
            for c in range(YN):
                nc.sync.dma_start(b2_rows[c * E:(c + 1) * E, :], exp_b2[0][:, c * BANK:(c + 1) * BANK]).then_inc(consts_landed, 16)
            nc.sync.dma_start(w_out_sb, w_out[0].rearrange("(k p) n -> p k n", p=P)).then_inc(w_out_landed, 16)

            def load_w1(pair, k, n):
                if n is not None:
                    sp.wait_ge(w1_used, n * KD + k - 3)
                nc.sync.dma_start(w1_ring[:, k % 4], exp_w1[0][bass.ds(pair * 2, 2), k * P:(k + 1) * P, :]
                                  .rearrange("e p n -> p e n")).then_inc(w1_landed[k % 4], 16)

            def load_w2(pair, s):
                for e in range(2):
                    nc.sync.dma_start(w2_ring[:, s, e], exp_w2[0][bass.ds(pair * 2 + e, 1), s * 2 * P:(s + 1) * 2 * P, :]
                                      .rearrange("e (k p) n -> p (e k) n", p=P)).then_inc(w2_landed[s], 16)

            def load_w1_half(r, pair, first):
                n = reg(nc.sync, r * PAIRS + pair, ROUNDS * PAIRS)
                for k in range(first, first + 4):
                    load_w1(pair, k, n)

            def load_w2_slots(r, pair, slots):
                n = reg(nc.sync, r * PAIRS + pair, ROUNDS * PAIRS)
                for s in slots:
                    sp.wait_ge(w2_used, n * 4 + s - 3)
                    load_w2(pair, s)

            def step(r, pair, early=0):
                load_w2_slots(r, pair - 1, range(early))
                load_w1_half(r, pair, 0)
                load_w2_slots(r, pair - 1, range(early, 4))
                load_w1_half(r, pair, 4)

            def pairs(r):
                if isinstance(r, int):
                    load_w1_half(r, 1, 0)
                    load_w1_half(r, 1, 4)
                    for i, early in enumerate(W2_EARLY):
                        step(r, 2 + i, early)
                    first = 2 + len(W2_EARLY)
                else:
                    load_w1_half(r, 0, 0)
                    load_w1_half(r, 0, 4)
                    first = 1
                with nc.sync.Fori(first, PAIRS) as pair:
                    step(r, pair)
                load_w2_slots(r, PAIRS - 1, range(4))

            for k in range(4):
                sp.wait_ge(w_mix_used, KD * (k + 1))
                load_w1(0, k, None)
            sp.wait_ge(z_conv_made, 1)
            load_w2(0, 3)
            sp.wait_ge(w_mix_used, IN_BLOCKS + KD)
            load_w2(0, 2)
            load_w2(0, 1)
            sp.wait_ge(w_mix_used, IN_BLOCKS + 2 * KD)
            load_w2(0, 0)
            load_w1_half(0, 0, 4)
            pairs(0)
            sp.wait_ge(counts_ready, 1)
            rounds_after_first(nc.sync, tokens_most(nc.sync), pairs)

            for t in range(NTILE):
                sp.wait_ge(final_ready[t], 1)
                dst = y_prompt[0][t * P:(t + 1) * P, :] if t < 2 else y_sample.rearrange("b t d -> (b t) d")
                nc.sync.dma_start(dst, x_norm[0:rows[t], t, :]).then_inc(stored, 16)
            sp.wait_ge(stored, 16 * (NTILE + 1))
            sp.wait_ge(cache_stored, 16 * (3 + NB))

        @block.tensor
        def _(pe):
            mm = nc.tensor.matmul

            def keep_awake(times, moving):
                for _ in range(times):
                    mm(psum[:, 6, 0:moving.shape[-1]], ident[:], moving, start=True, stop=True)

            pe.wait_ge(consts_made, 1)
            keep_awake(9, ident[:])
            pe.wait_ge(vecs_landed, 16 * 4)
            nc.tensor.transpose(psum[:, 0, 0:4 * KD], vec_rows[:], ident[0:4 * KD, 0:4 * KD]).then_inc(front_t, 1)

            keep_awake(12, ident[:])
            pe.wait_ge(scaled, NTILE)
            pe.wait_ge(front_t_read, 1)
            for k in range(KD):
                for t in range(NTILE):
                    last = nc.tensor.transpose(psum[:, k, t * P:t * P + rows[t]],
                                               x_norm[0:rows[t], t, k * P:(k + 1) * P],
                                               ident[0:rows[t], 0:rows[t]])
                last.then_inc(x_t_ready, 1)

            for j in range(4):
                if j == 1:
                    pe.wait_ge(states_landed, 16 * 2)
                    for i in range(KC):
                        last = nc.tensor.transpose(psum[:, 4, 16 * i:16 * i + NB * CB], conv_rows[:, i * P:(i + 1) * P],
                                                   ident[0:NB * CB, 0:NB * CB])
                    last.then_inc(front_t, 1)
                    for i in range(NG):
                        last = nc.tensor.transpose(psum[:, 5, P * i:P * i + NB * PB], pool_rows[:, i * P:(i + 1) * P],
                                                   ident[0:NB * PB, 0:NB * PB])
                    last.then_inc(front_t, 1)
                    pe.wait_ge(front_t_read, 3)
                if j >= 2:
                    pe.wait_ge(proj_read, j - 1)
                for k in range(KD):
                    if j == 0 and k == 0:
                        pe.wait_ge(x_low_ready, 4)
                    elif j == 0 and k >= 4:
                        pe.wait_ge(x_low_ready, k + 1)
                    if j == 3 and k == 2:
                        pe.wait_ge(last_ready, 1)
                        for i in range(KC):
                            nc.tensor.transpose(psum[0:CB, 0, i * P:(i + 1) * P], u_pad[:, i, NP:NP + CB], ident[:])
                            nc.tensor.transpose(psum[0:NB * CB, 1, i * P:(i + 1) * P], u_last[:, i, :], ident[:])
                            nc.tensor.transpose(psum[0:PB, 2, i * P:(i + 1) * P], v_pad[:, i, NP:NP + PB], ident[:])
                            last = nc.tensor.transpose(psum[0:NS, 3, i * P:(i + 1) * P], v_last[:, i, :], ident[:])
                        last.then_inc(cache_ready, 1)
                    if j == 3 and k == 6:
                        pe.wait_ge(pooled, 1)
                        pe.wait_ge(cache_read, 1)
                        pe.wait_ge(consts_landed, 16 * 10)
                        for g in range(NG):
                            last = mm(psum[:, g, 0:T], pool_f[:, g, :], p_t[:, g, :], start=True, stop=True)
                        last.then_inc(z_pool_ready, 1)
                    pe.wait_ge(w_low_ready, KD * j + k + 1)
                    for m in range(KC):
                        cols = slice(m * P, (m + 1) * P)
                        w_h, w_l = w_high[:, (KD * j + k) % 3, cols], w_low[:, j, k, cols]
                        x_h, x_l = x_parts[:, 0, k, :], x_parts[:, 1, k, :]
                        out = psum[:, 4 * (j % 2) + m, 0:T]
                        mm(out, w_h, x_h, start=(k == 0), stop=False)
                        mm(out, w_h, x_l, start=False, stop=False)
                        last = mm(out, w_l, x_h, start=False, stop=(k == KD - 1))
                    last.then_inc(w_mix_used, 1)

            pe.wait_ge(z_pool_low_ready, NG)
            for i, (k, n) in enumerate(OUT_BLOCKS):
                if i == KD:
                    pe.wait_ge(z_conv_low_ready, 1)
                pe.wait_ge(w_low_ready, IN_BLOCKS + i + 1)
                w_h = w_high[:, (IN_BLOCKS + i) % 3, :]
                w_l = w_out_low[:, k, n * BANK:(n + 1) * BANK]
                first, final = k == 4, k == 3
                for t in MIX_ORDER:
                    if i == 0 and t == MIX_ORDER[2]:
                        pe.wait_ge(z_conv_made, 1)
                    z = z_pool_parts[:, k - KC] if k >= KC else z_conv_parts[:, k]
                    z_h = z[:, t * P:t * P + rows[t]]
                    bank = psum[:, mix_bank(t, n), :]
                    if t == 2:
                        mm(bank[0:2 * NS], z[:, NP:T + NS], w_h, start=first, stop=final, skip_group_check=True)
                        last = mm(bank[0:NS], z_h, w_l, start=False, stop=final, skip_group_check=True)
                    else:
                        z_l = z[:, T + NS + t * P:T + NS + (t + 1) * P]
                        mm(bank, z_h, w_h, start=first, stop=False)
                        mm(bank, z_h, w_l, start=False, stop=False)
                        last = mm(bank, z_l, w_h, start=False, stop=final)
                    if final and t != MIX_ORDER[2]:
                        last.then_inc(mixed, 1)
                last.then_inc(w_mix_used, 1)

            keep_awake(3, ident[:])
            for k in range(KD):
                for t in range(NTILE):
                    if k == 0:
                        pe.wait_ge(residual, YN * NTILE)
                    last = nc.tensor.transpose(psum[:, k, t * P:t * P + rows[t]],
                                               x_acc[0:rows[t], t, k * P:(k + 1) * P],
                                               ident[0:rows[t], 0:rows[t]])
                last.then_inc(x_t_ready, 1)
            for k in range(KD):
                pe.wait_ge(x_t_act if k % 2 else x_t_dve, k // 2 + 1)
                last = mm(psum[(k % 4) * E:(k % 4 + 1) * E, 0, 0:T], router_g[:, k, :], x_t[:, k, :],
                          start=(k < 4), stop=(k >= 4))
            last.then_inc(logit_parts_ready, 1)
            keep_awake(1, x_t[:, 0, :])
            pe.wait_ge(logit_parts_read, 1)
            for t in range(NTILE):
                last = mm(psum[0:rows[t], 1, t * E:(t + 1) * E], logit_parts[:, t * P:t * P + rows[t]],
                          pick_table[:, 0:E], start=True, stop=True)
            last.then_inc(logits_ready, 1)

            def add_b1(blocks):
                for c in blocks:
                    last = mm(psum[:, c, :], pick_b1[c * E:(c + 1) * E], b1_rows[c * E:(c + 1) * E, :],
                              start=True, stop=False, skip_group_check=True)
                return last

            pe.wait_ge(picked_b1, 1)
            keep_awake(1, x_t[:, 0, :])
            add_b1((0, 2))
            keep_awake(2, x_t[:, 0, :])
            pe.wait_ge(mask_ready, 1)
            mm(psum[:, 7, 0:(NTILE + 1) * E], before[:], mask[:], start=True, stop=False)
            for t in range(1, NTILE + 1):
                last = mm(psum[:, 7, t * E:(NTILE + 1) * E], ones[:], mask[:, 0:NTILE + 1 - t, :],
                          start=False, stop=(t == NTILE))
            last.then_inc(ranks_ready, 1)
            add_b1((1, 3))

            def gather(blocks, done):
                for k in blocks:
                    for t in range(NTILE):
                        last = mm(psum[:, 4 + k // 4, (k % 4) * P:(k % 4 + 1) * P],
                                  x_norm[0:rows[t], t, k * P:(k + 1) * P], place[0:rows[t], t],
                                  start=(t == 0), stop=(t == NTILE - 1))
                last.then_inc(done, 1)

            def turn_back():
                for t in range(NTILE):
                    last = nc.tensor.transpose(psum[:, 6, t * P:t * P + rows[t]], gated[0:rows[t], t],
                                               ident[0:rows[t], 0:rows[t]])
                last.then_inc(back_ready, 1)

            def first_product(n, blocks):
                for k in blocks:
                    pe.wait_ge(w1_landed[k % 4], 32 * n + 16 * (k // 4) + 16)
                    for c in range(W1N):
                        for e in range(2):
                            last = mm(psum[e * SLOTS:(e + 1) * SLOTS, c, :], gathered_t[:, k, e, :],
                                      w1_ring[:, k % 4, e, c * BANK:(c + 1) * BANK],
                                      start=False, stop=(k == KD - 1), skip_group_check=True)
                    last.then_inc(w1_used, 1)

            def pair_steps(n, final):
                pe.wait_ge(gathered_read, 2 * n + 2)
                first_product(n, range(4, KD))
                if not final:
                    pe.wait_ge(place_ready, n + 2)
                    pe.wait_ge(y_read, 2 * n + 2)
                    gather(range(4), gathered)
                    gather(range(4, KD), gathered)
                pe.wait_ge(back_read, n + 1)
                pe.wait_ge(spread_read, 6 * n + 6)

                def transpose_h(half_h):
                    pe.wait_ge(h_ready, 2 * n + half_h + 1)
                    for k in range(4):
                        last = nc.tensor.transpose(psum[:, 6 + half_h, k * P:(k + 1) * P],
                                                   hidden[:, 0, half_h, k * P:(k + 1) * P], ident[:])
                    last.then_inc(h_t_ready, 1)

                def add_b2():
                    pe.wait_ge(picked_b2, n + 1)
                    for c in range(YN):
                        mm(psum[:, 4 + c, :], pick_b2[c * E:(c + 1) * E], b2_rows[c * E:(c + 1) * E, :],
                           start=True, stop=False, skip_group_check=True)

                if final:
                    pe.wait_ge(y_read, 2 * n + 2)
                    add_b2()
                    transpose_h(0)
                else:
                    transpose_h(0)
                    transpose_h(1)
                    pe.wait_ge(picked_b1, n + 2)
                    add_b1(range(W1N))
                    pe.wait_ge(gathered_read, 2 * n + 4)
                    first_product(n + 1, range(4))
                    add_b2()
                for s in range(4):
                    if final and s == 2:
                        transpose_h(1)
                    if s % 2 == 0:
                        pe.wait_ge(h_t_read, 2 * n + s // 2 + 1)
                    pe.wait_ge(w2_landed[s], 32 * n + 32)
                    for c in range(YN):
                        for k in (2 * s, 2 * s + 1):
                            for e in range(2):
                                last = mm(psum[e * SLOTS:(e + 1) * SLOTS, 4 + c, :], h_t[:, k, e, :],
                                          w2_ring[:, s, e, k % 2, c * BANK:(c + 1) * BANK],
                                          start=False, stop=(k == KD - 1), skip_group_check=True)
                        if s == 3 and c < YN - 1:
                            last.then_inc(y_part, 1)
                    last.then_inc(w2_used, 1)
                for j in range(YN * NTILE):
                    c, t = divmod(j, NTILE)
                    if t == 0:
                        pe.wait_ge(y_read, 2 * n + 3 + c)
                    if j < 2:
                        pe.wait_ge(h_t_read, 2 * n + 2)
                    else:
                        pe.wait_ge(spread_read, 6 * n + 5 + j)
                    last = mm(psum[0:rows[t], 6 + j % 2, :], back[:, t * P:t * P + rows[t]],
                              y_slots[:, c, :], start=True, stop=True)
                    last.then_inc(spread, 1)
                if not final:
                    pe.wait_ge(gated_ready, n + 2)
                    pe.wait_ge(spread_read, 6 * n + 11)
                    turn_back()

            def round_of(r):
                n0 = reg(nc.tensor, r * PAIRS, ROUNDS * PAIRS)
                if isinstance(r, int):
                    pe.wait_ge(x_norm_ready, NTILE)
                else:
                    pe.wait_ge(y_read, 2 * n0 + 2)
                    pe.wait_ge(spread_read, 6 * n0 + 6)
                    pe.wait_ge(picked_b1, n0 + 1)
                    add_b1(range(W1N))
                pe.wait_ge(place_ready, n0 + 1)
                gather(range(2), first_gathered)
                if isinstance(r, int):
                    keep_awake(1, x_t[:, 0, :])
                pe.wait_ge(first_copied, r + 1)
                first_product(n0, range(2))
                gather(range(2, 4), gathered)
                pe.wait_ge(gathered_read, 2 * n0 + 1)
                first_product(n0, range(2, 4))
                gather(range(4, KD), gathered)
                pe.wait_ge(gated_ready, n0 + 1)
                turn_back()
                with nc.tensor.Fori(0, PAIRS - 1) as pair:
                    pair_steps(reg(nc.tensor, r * PAIRS + pair, ROUNDS * PAIRS), False)
                pair_steps(reg(nc.tensor, r * PAIRS + PAIRS - 1, ROUNDS * PAIRS), True)

            round_of(0)
            pe.wait_ge(counts_ready, 1)
            rounds_after_first(nc.tensor, tokens_most(nc.tensor), round_of)

        @block.scalar
        def _(act):
            A = nc.scalar.activation

            nc.scalar.dma_start(vec_rows[G_MIX:G_MIX + KD, :],
                                norm_mix_g[0].rearrange("(k c) -> k c", c=P)).then_inc(vecs_landed, 16)
            act.wait_ge(presets_made, 1)
            A(warm[:], half[:, 0:1], ACT.Square)
            for t in range(NTILE):
                if t == 1:
                    continue
                act.wait_ge(x_landed[t], 16)
                A(x_norm[0:rows[t], t, :], x_acc[0:rows[t], t, :], ACT.Square,
                  accum_out=sumsq[0:rows[t], 0, t:t + 1]).then_inc(squares, 1)
            act.wait_ge(rms_ready, 1)
            act.wait_ge(squares, NTILE)
            A(x_norm[:, 1, :], x_acc[:, 1, :], ACT.Copy, scale=rms[:, 0, 1:2]).then_inc(scaled, 1)
            def high_parts(first, end):
                for c in range(first, end):
                    if c >= IN_BLOCKS:
                        k, n = OUT_BLOCKS[c - IN_BLOCKS]
                        block = w_out_sb[:, k, n * BANK:(n + 1) * BANK]
                    else:
                        block = w_in_sb[:, c // KD, c % KD, :]
                    if c == 0:
                        act.wait_ge(w_in_begun, 16)
                    elif c == IN_BLOCKS:
                        act.wait_ge(w_out_landed, 16)
                    elif c < IN_BLOCKS and (c % KD == 0 or c == 4):
                        act.wait_ge(w_in_landed[c // KD], 16)
                    if c >= 3:
                        act.wait_ge(w_mix_used, c - 2)
                    A(w_high[:, c % 3, :], block, ACT.Copy).then_inc(w_high_ready, 1)

            high_parts(0, 2)
            act.wait_ge(front_t_read, 1)
            for k in range(KD):
                act.wait_ge(x_t_ready, k + 1)
                A(x_parts[:, 0, k, :], psum[:, k, 0:T], ACT.Copy,
                  scale=vecs[:, G_MIX + k:G_MIX + k + 1]).then_inc(x_high_ready, 1)
            high_parts(2, 3)
            nc.scalar.dma_start(new_pool_sample[0][:, 0:PB - NT, :], state_pool[0][:, NT:PB, :]).then_inc(stored, 16)
            high_parts(3, KD + 2)
            act.wait_ge(w_mix_used, KD)
            A(c_gate, psum[:, 0:4, 0:T], ACT.Copy).then_inc(proj_read, 1)
            high_parts(KD + 2, 3 * KD + 2)
            act.wait_ge(w_mix_used, 3 * KD)
            act.wait_ge(front_t_read, 5)
            A(v_pad[:, :, PB:PB + NP], psum[:, 0:4, 0:NP], ACT.Copy)
            for j in range(NG):
                last = A(v_pad[:, j, PS:PL].rearrange("p (b t) -> p b t", b=NB)[:, :, PB:PB + NT],
                         psum[:, j, NP:T].rearrange("p (b t) -> p b t", b=NB), ACT.Copy)
            last.then_inc(v_ready, 1)
            high_parts(3 * KD + 2, 3 * KD + 5)
            act.wait_ge(cache_ready, 1)
            A(cache_rows[0:CB, 0, :], psum[0:CB, 0, :], ACT.Copy)
            A(cache_rows[0:NB * CB, 1, :], psum[0:NB * CB, 1, :], ACT.Copy)
            A(cache_rows[0:PB, 2, :], psum[0:PB, 2, :], ACT.Copy)
            A(cache_rows_v[:], psum[0:NS, 3, :], ACT.Copy).then_inc(cache_read, 1)
            high_parts(3 * KD + 5, 4 * KD)
            act.wait_ge(z_pool_ready, 1)
            for g in range(NG):
                A(z_pool_parts[:, g, HIGH], psum[:, g, 0:T], ACT.Copy,
                  scale=vecs[:, SCALE + g:SCALE + g + 1]).then_inc(z_pool_high_ready, 1)
            high_parts(IN_BLOCKS, IN_BLOCKS + 2)
            act.wait_ge(cache_read, 1)
            stores = [(new_conv_prompt[0, 0], cache_rows[0:CB, 0, :]),
                      (new_conv_sample[0].rearrange("b j c -> (b j) c"), cache_rows[0:NB * CB, 1, :]),
                      (new_pool_prompt[0, 0], cache_rows[0:PB, 2, :])]
            stores += [(new_pool_sample[0, b, PB - NT:PB, :], cache_rows_v[b * NT:(b + 1) * NT, :])
                       for b in range(NB)]
            for i, (dst, src) in enumerate(stores):
                nc.scalar.dma_start(dst, src).then_inc(cache_stored, 16)
                high_parts(IN_BLOCKS + 2 + i, IN_BLOCKS + 3 + i)
            high_parts(IN_BLOCKS + 2 + len(stores), IN_BLOCKS + len(OUT_BLOCKS))
            act.wait_ge(cache_stored, 16 * (3 + NB))
            for n in range(YN):
                for i, t in enumerate(MIX_ORDER):
                    act.wait_ge(residual, NTILE * n + i + 1)
                    own = (slice(0, rows[t]), t, slice(n * BANK, (n + 1) * BANK))
                    total = sumsq_right[0:rows[t], t:t + 1] if n else sumsq[0:rows[t], 1, t:t + 1]
                    A(x_norm[own], x_acc[own], ACT.Square, accum_out=total).then_inc(squares, 1)
            for k in range(1, KD, 2):
                act.wait_ge(x_t_ready, KD + k + 1)
                A(x_t[:, k, :], psum[:, k, 0:T], ACT.Copy).then_inc(x_t_act, 1)
            act.wait_ge(logit_parts_ready, 1)
            A(logit_parts, psum[:, 0, 0:T], ACT.Copy).then_inc(logit_parts_read, 1)
            act.wait_ge(rms_ready, 2)
            act.wait_ge(squares, NORM_SQUARES[1])
            for t in (1, 2):
                A(x_norm[0:rows[t], t, :], x_acc[0:rows[t], t, :], ACT.Copy,
                  scale=rms[0:rows[t], 1, t:t + 1]).then_inc(scaled, 1)
            act.wait_ge(shifted_ready, 1)
            A(shifted[:], shifted[:], ACT.Exp).then_inc(exp_ready, 1)
            nc.scalar.sem_inc(y_read, 2)
            act.wait_ge(x_norm_ready, NTILE)
            nc.scalar.dma_start(gain[:], final_norm_g[None, :].to_broadcast([P, D])).then_inc(g_final_landed, 16)

            def copy_gathered(n):
                for b in range(2):
                    act.wait_ge(gathered, 2 * n + b + 1)
                    A(routed[:, 0, b * BANK:(b + 1) * BANK], psum[:, 4 + b, :], ACT.Copy).then_inc(gathered_read, 1)

            def copy_back(n):
                act.wait_ge(back_ready, n + 1)
                A(back[:], psum[:, 6, 0:T], ACT.Copy).then_inc(back_read, 1)

            def pair_steps(n, final):
                for b in range(2):
                    act.wait_ge(gate_ready, 2 * n + b + 1)
                    A(hidden[:, 2, b, :], hidden[:, 0, b, :], ACT.Sigmoid, scale=SWIGLU_ALPHA).then_inc(sig_ready, 1)
                if not final:
                    copy_gathered(n + 1)
                for b in range(2):
                    act.wait_ge(h_t_ready, 2 * n + b + 1)
                    A(routed[:, 1, b * BANK:(b + 1) * BANK], psum[:, 6 + b, :], ACT.Copy).then_inc(h_t_read, 1)
                for c in range(YN):
                    if c < YN - 1:
                        act.wait_ge(y_part, (YN - 1) * n + c + 1)
                    else:
                        act.wait_ge(w2_used, 4 * n + 4)
                    A(y_slots[:, c, :], psum[:, 4 + c, :], ACT.Copy).then_inc(y_read, 1)
                if not final:
                    copy_back(n + 1)

            def round_of(r):
                n0 = reg(nc.scalar, r * PAIRS, ROUNDS * PAIRS)
                act.wait_ge(first_gathered, r + 1)
                A(routed[:, 0, 0:2 * P], psum[:, 4, 0:2 * P], ACT.Copy).then_inc(first_copied, 1)
                act.wait_ge(gathered, 2 * n0 + 1)
                A(routed[:, 0, 2 * P:4 * P], psum[:, 4, 2 * P:4 * P], ACT.Copy).then_inc(gathered_read, 1)
                act.wait_ge(gathered, 2 * n0 + 2)
                A(routed[:, 0, 4 * P:8 * P], psum[:, 5, :], ACT.Copy).then_inc(gathered_read, 1)
                copy_back(n0)
                with nc.scalar.Fori(0, PAIRS - 1) as pair:
                    pair_steps(reg(nc.scalar, r * PAIRS + pair, ROUNDS * PAIRS), False)
                pair_steps(reg(nc.scalar, r * PAIRS + PAIRS - 1, ROUNDS * PAIRS), True)

            round_of(0)
            act.wait_ge(counts_ready, 1)
            rounds_after_first(nc.scalar, tokens_most(nc.scalar), round_of)

            act.wait_ge(moe_done, 1)
            for t in (0, 2):
                A(x_norm[0:rows[t], t, :], x_acc[0:rows[t], t, :], ACT.Square,
                  accum_out=sumsq[0:rows[t], 2, t:t + 1]).then_inc(squares, 1)
            act.wait_ge(rms_ready, 3)
            act.wait_ge(squares, NORM_SQUARES[2])
            for t in (2, 1):
                A(x_norm[0:rows[t], t, :], x_acc[0:rows[t], t, :], ACT.Copy, scale=rms[0:rows[t], 2, t:t + 1]).then_inc(final_scaled, 1)

        @block.vector
        def _(dve):
            V = nc.vector
            step = Counter(dve_step)

            def then(ins):
                step.inc(ins)
                dve.wait_ge(dve_step, step.now())

            V.memset(sumsq[:], 1.0)
            V.memset(sumsq_right[:], 0.0)
            V.memset(half[:], -0.5)
            V.memset(logits[:], 0.0)
            V.memset(rank[:], 0.0)
            V.memset(combine[:], 0.0)
            V.memset(mask[:, NTILE, :], 0.0)
            V.memset(pick_table[:], 0.0).then_inc(presets_made, 1)
            dve.wait_ge(presets_made, 1)
            def squares_of(i):
                V.tensor_tensor_reduce(out=x_norm[:, 1, :], in0=x_acc[:, 1, :], in1=x_acc[:, 1, :], scale=1.0,
                                       scalar=0.0, op0=ALU.mult, op1=ALU.add,
                                       accum_out=sumsq[:, i, 1:2]).then_inc(squares, 1)

            dve.wait_ge(x_landed[1], 16)
            squares_of(0)
            dve.wait_ge(front_t, 1)
            V.tensor_copy(vecs[:], psum[:, 0, 0:4 * KD]).then_inc(front_t_read, 1)
            dve.wait_ge(rms_ready, 1)
            for t in (0, 2):
                V.tensor_scalar(x_norm[0:rows[t], t, :], x_acc[0:rows[t], t, :], rms[0:rows[t], 0, t:t + 1],
                                None, ALU.mult).then_inc(scaled, 1)
            dve.wait_ge(front_t_read, 1)
            for k in range(KD):
                dve.wait_ge(x_high_ready, k + 1)
                V.scalar_tensor_tensor(out=x_parts[:, 1, k, :], in0=psum[:, k, 0:T],
                                       scalar=vecs[:, G_MIX + k:G_MIX + k + 1],
                                       in1=x_parts[:, 0, k, :].bitcast(F32), op0=ALU.mult,
                                       op1=ALU.subtract).then_inc(x_low_ready, 1)
            dve.wait_ge(front_t, 3)
            for j in range(KC):
                last = V.tensor_copy(u_pad[:, j, CS:CL].rearrange("p (b t) -> p b t", b=NB)[:, :, 0:CB],
                                     psum[:, 4, 16 * j:16 * j + NB * CB].rearrange("p (b t) -> p b t", b=NB))
            last.then_inc(front_t_read, 1)
            for j in range(NG):
                last = V.tensor_copy(v_pad[:, j, PS:PL].rearrange("p (b t) -> p b t", b=NB)[:, :, 0:PB],
                                     psum[:, 5, P * j:P * j + NB * PB].rearrange("p (b t) -> p b t", b=NB))
            last.then_inc(front_t_read, 1)
            V.memset(u_pad[:, :, 0:CB], 0.0).then_inc(front_t_read, 1)
            V.memset(v_pad[:, :, 0:PB], 0.0).then_inc(front_t_read, 1)
            dve.wait_ge(consts_made, 1)
            for c in range(W1N):
                last = V.tensor_copy(pick_table[c * E:(c + 1) * E, 0:E], ident[c * E:(c + 1) * E, c * E:(c + 1) * E])
            then(last)

            def picked(pair):
                return pick_table[:, bass.ds(pair * 2, 2)].unsqueeze(2).to_broadcast([P, 2, SLOTS])

            V.tensor_copy(pick_b1[:], picked(0)).then_inc(picked_b1, 1)
            dve.wait_ge(consts_made, 2)
            then(V.reciprocal(ramp[:], ramp[:]))
            for g, w in enumerate(WINDOWS):
                last = V.tensor_scalar(fix[:, g, :], ramp[:], float(w), 1.0, ALU.mult, ALU.max)
            dve.wait_ge(consts_landed, 16 * 10)
            for k in range(KD):
                last = V.tensor_scalar(router_g[:, k, :], router_f[:, k, :], vecs[:, G_FFN + k:G_FFN + k + 1], None,
                                       ALU.mult)
            then(last)

            dve.wait_ge(proj_read, 1)
            dve.wait_ge(w_mix_used, 2 * KD)
            V.tensor_tensor(u_pad[:, :, CB:CB + NP], psum[:, 4:8, 0:NP], c_gate[:, :, 0:NP], ALU.mult)
            for j in range(KC):
                last = V.tensor_tensor(u_pad[:, j, CS:CL].rearrange("p (b t) -> p b t", b=NB)[:, :, CB:CB + NT],
                                       psum[:, 4 + j, NP:T].rearrange("p (b t) -> p b t", b=NB),
                                       c_gate[:, j, NP:T].rearrange("p (b t) -> p b t", b=NB), ALU.mult)
            last.then_inc(proj_read, 1)
            dve.wait_ge(proj_read, 2)
            for w in range(3):
                for j in range(KC):
                    wcol = vecs[:, CONV_W + KC * w + j:CONV_W + KC * w + j + 1]
                    src = u_pad[:, j, w:w + CY]
                    if w == 0:
                        last = V.tensor_scalar(conv_y[:, j, 0:CY], src, wcol, None, ALU.mult)
                    else:
                        last = V.scalar_tensor_tensor(out=conv_y[:, j, 0:CY], in0=src, scalar=wcol,
                                                      in1=conv_y[:, j, 0:CY], op0=ALU.mult, op1=ALU.add)
                then(last)
            dve.wait_ge(v_ready, 1)
            V.tensor_copy(u_last.rearrange("p k (b t) -> p k b t", b=NB),
                          u_pad[:, :, CS:CL].rearrange("p k (b t) -> p k b t", b=NB)[:, :, :, NT:NT + CB])
            V.tensor_copy(v_last.rearrange("p k (b t) -> p k b t", b=NB),
                          v_pad[:, :, PS:PL].rearrange("p k (b t) -> p k b t", b=NB)[:, :, :, PB:PB + NT]).then_inc(last_ready, 1)
            then(V.tensor_tensor(sum_a[:, :, 1:PL], v_pad[:, :, 1:PL], v_pad[:, :, 0:PL - 1], ALU.add))
            then(V.tensor_tensor(sum_b[:, 1:4, 3:PL], sum_a[:, 1:4, 3:PL], sum_a[:, 1:4, 1:PL - 2], ALU.add))
            then(V.tensor_tensor(sum_a[:, 2:4, 7:PL], sum_b[:, 2:4, 7:PL], sum_b[:, 2:4, 3:PL - 4], ALU.add))
            then(V.tensor_tensor(sum_b[:, 3, 15:PL], sum_a[:, 3, 15:PL], sum_a[:, 3, 7:PL - 8], ALU.add))
            sums = (sum_a, sum_b, sum_a, sum_b)
            for g in range(NG):
                last = V.tensor_tensor(sums[g][:, g, PB:PB + 16], sums[g][:, g, PB:PB + 16], fix[:, g, :], ALU.mult)
            then(last)
            for g, w in enumerate(WINDOWS):
                V.scalar_tensor_tensor(out=p_t[:, g, 0:NP], in0=sums[g][:, g, PB:PB + NP], scalar=1.0 / w,
                                       in1=v_pad[:, g, PB:PB + NP], op0=ALU.mult, op1=ALU.subtract)
                tail_s = sums[g][:, g, PS:PL].rearrange("p (b t) -> p b t", b=NB)[:, :, PB:PB + NT]
                tail_v = v_pad[:, g, PS:PL].rearrange("p (b t) -> p b t", b=NB)[:, :, PB:PB + NT]
                last = V.scalar_tensor_tensor(out=p_t[:, g, NP:T].rearrange("p (b t) -> p b t", b=NB), in0=tail_s,
                                              scalar=1.0 / w, in1=tail_v, op0=ALU.mult, op1=ALU.subtract)
            last.then_inc(pooled, 1)
            for g in range(NG):
                dve.wait_ge(z_pool_high_ready, g + 1)
                for low, own in ((LOW_SAMPLE, slice(NP, T)), (LOW_PROMPT, slice(0, NP))):
                    last = V.scalar_tensor_tensor(out=z_pool_parts[:, g, low], in0=psum[:, g, own],
                                                  scalar=vecs[:, SCALE + g:SCALE + g + 1],
                                                  in1=z_pool_parts[:, g, own].bitcast(F32),
                                                  op0=ALU.mult, op1=ALU.subtract)
                last.then_inc(z_pool_low_ready, 1)
            dve.wait_ge(w_mix_used, IN_BLOCKS)
            V.tensor_tensor(z_conv[:, :, 0:NP], psum[:, 4:8, 0:NP], conv_y[:, :, 0:NP], ALU.mult)
            for j in range(KC):
                last = V.tensor_tensor(z_conv[:, j, NP:T].rearrange("p (b t) -> p b t", b=NB),
                                       psum[:, 4 + j, NP:T].rearrange("p (b t) -> p b t", b=NB),
                                       conv_y[:, j, CS:CL].rearrange("p (b t) -> p b t", b=NB)[:, :, 0:NT], ALU.mult)
            last.then_inc(z_conv_made, 1)
            dve.wait_ge(z_conv_made, 1)
            V.tensor_copy(z_conv_parts[:, :, HIGH], z_conv).then_inc(z_conv_high_ready, 1)
            dve.wait_ge(z_conv_high_ready, 1)
            for low, own in ((LOW_SAMPLE, slice(NP, T)), (LOW_PROMPT, slice(0, NP))):
                last = V.tensor_tensor(z_conv_parts[:, :, low], z_conv[:, :, own],
                                       z_conv_parts[:, :, own].bitcast(F32), ALU.subtract)
            last.then_inc(z_conv_low_ready, 1)
            for n in range(YN):
                for i, t in enumerate(MIX_ORDER):
                    if t == MIX_ORDER[2]:
                        dve.wait_ge(w_mix_used, IN_BLOCKS + OUT_BLOCKS.index((KC - 1, n)) + 1)
                    else:
                        dve.wait_ge(mixed, (NTILE - 1) * n + i + 1)
                    own = x_acc[0:rows[t], t, n * BANK:(n + 1) * BANK]
                    for q in range(2 if t == 2 else 1):
                        last = V.tensor_tensor(own, own, psum[q * NS:q * NS + rows[t], mix_bank(t, n), :], ALU.add)
                        if t == 2 and q < 1:
                            then(last)
                    last.then_inc(residual, 1)
            for k in range(0, KD, 2):
                dve.wait_ge(x_t_ready, KD + k + 1)
                V.tensor_copy(x_t[:, k, :], psum[:, k, 0:T]).then_inc(x_t_dve, 1)

            dve.wait_ge(rms_ready, 2)
            dve.wait_ge(residual, YN * NTILE)
            dve.wait_ge(consts_landed, 16 * 10)
            V.scalar_tensor_tensor(out=x_norm[:, 0, :], in0=x_acc[:, 0, :], scalar=rms[:, 1, 0:1], in1=gain[:],
                                   op0=ALU.mult, op1=ALU.mult).then_inc(x_norm_ready, 1)
            dve.wait_ge(logits_ready, 1)
            for t in range(NTILE):
                last = V.scalar_tensor_tensor(out=logits[0:rows[t], t, :], in0=psum[0:rows[t], 1, t * E:(t + 1) * E],
                                              scalar=rms[0:rows[t], 1, t:t + 1], in1=bias_e[0:rows[t], :],
                                              op0=ALU.mult, op1=ALU.add)
            then(last)
            for t in range(NTILE):
                last = V.max(top8[:, t, :], logits[:, t, :])
            then(last)
            V.tensor_tensor(shifted[:], logits[:], top8[:, :, 0:1].to_broadcast([P, NTILE, E]),
                            ALU.subtract).then_inc(shifted_ready, 1)
            for t in range(NTILE):
                last = V.max_index(top_at[:, t, :], top8[:, t, :], logits[:, t, :])
            then(last)
            then(V.tensor_copy(top_f[:], top_at[:]))
            dve.wait_ge(consts_made, 2)
            for t in range(NTILE):
                last = V.tensor_tensor(match[:, t], expert_id[:].unsqueeze(2).to_broadcast([P, E, TOP_K]),
                                       top_f[:, t, 0:TOP_K].unsqueeze(1).to_broadcast([P, E, TOP_K]), ALU.is_equal)
            then(last)
            then(V.tensor_reduce(mask[:, 0:NTILE, :], match[:], AX.X, ALU.max))
            V.memset(mask[32:64, 2, :], 0.0)
            V.memset(mask[64:128, 2, :], 0.0).then_inc(mask_ready, 1)
            dve.wait_ge(mask_ready, 1)
            dve.wait_ge(exp_ready, 1)
            then(V.tensor_tensor(combine[:, :, 0:E], shifted[:], mask[:, 0:NTILE, :], ALU.mult))
            then(V.tensor_reduce(denom[:], combine[:, :, 0:E], AX.X, ALU.add))
            V.memset(denom[32:64, 2:3], 1.0)
            then(V.memset(denom[64:128, 2:3], 1.0))
            then(V.reciprocal(denom[:], denom[:]))
            V.tensor_tensor(combine[:, :, 0:E], combine[:, :, 0:E], denom[:].unsqueeze(2).to_broadcast([P, NTILE, E]),
                            ALU.mult).then_inc(combine_ready, 1)
            dve.wait_ge(combine_ready, 1)
            dve.wait_ge(ranks_ready, 1)
            then(V.scalar_tensor_tensor(out=rank[:, :, 0:E],
                                        in0=psum[:, 7, 0:NTILE * E].rearrange("p (t e) -> p t e", t=NTILE),
                                        scalar=1.0, in1=mask[:, 0:NTILE, :], op0=ALU.add, op1=ALU.mult))
            dve.sem_inc(spread_read, NTILE * YN)

            def build(pair, n):
                def own(table):
                    return table[:, :, bass.ds(pair * 2, 2)].unsqueeze(3).to_broadcast([P, NTILE, 2, SLOTS])

                ids = slot_id[:].unsqueeze(1).unsqueeze(1).to_broadcast([P, NTILE, 2, SLOTS])
                V.tensor_tensor(place[:], ids, own(rank), ALU.is_equal).then_inc(place_ready, 1)
                dve.wait_ge(place_ready, n + 1)
                V.tensor_tensor(gated[:], place[:], own(combine), ALU.mult).then_inc(gated_ready, 1)

            def pair_steps(pair, n, final):
                if not final:
                    dve.wait_ge(back_ready, n + 1)
                    nxt = reg(nc.vector, pair + 1, PAIRS)
                    V.tensor_copy(pick_b1[:], picked(nxt)).then_inc(picked_b1, 1)
                    build(nxt, n + 1)
                V.tensor_copy(pick_b2[:], picked(pair)).then_inc(picked_b2, 1)
                dve.wait_ge(w1_used, KD * n + KD)
                for b in range(2):
                    V.tensor_scalar(hidden[:, 0, b, :], psum[:, b, :], SWIGLU_LIMIT, None,
                                    ALU.min).then_inc(gate_ready, 1)
                for b in range(2):
                    V.tensor_scalar(hidden[:, 1, b, :], psum[:, 2 + b, :], SWIGLU_LIMIT, -SWIGLU_LIMIT,
                                    ALU.min, ALU.max).then_inc(lin_step, 1)
                    dve.wait_ge(gate_ready, 2 * n + b + 1)
                    dve.wait_ge(lin_step, 4 * n + 2 * b + 1)
                    V.scalar_tensor_tensor(out=hidden[:, 1, b, :], in0=hidden[:, 1, b, :], scalar=1.0,
                                           in1=hidden[:, 0, b, :], op0=ALU.add, op1=ALU.mult).then_inc(lin_step, 1)
                    dve.wait_ge(lin_step, 4 * n + 2 * b + 2)
                    dve.wait_ge(sig_ready, 2 * n + b + 1)
                    V.tensor_tensor(hidden[:, 0, b, :], hidden[:, 1, b, :], hidden[:, 2, b, :],
                                    ALU.mult).then_inc(h_ready, 1)
                for j in range(YN * NTILE):
                    c, t = divmod(j, NTILE)
                    dve.wait_ge(spread, 6 * n + j + 1)
                    V.tensor_tensor(x_acc[0:rows[t], t, c * BANK:(c + 1) * BANK],
                                    x_acc[0:rows[t], t, c * BANK:(c + 1) * BANK],
                                    psum[0:rows[t], 6 + j % 2, :], ALU.add).then_inc(spread_read, 1)

            def round_of(r):
                n0 = reg(nc.vector, r * PAIRS, ROUNDS * PAIRS)
                if not isinstance(r, int):
                    V.tensor_copy(pick_b1[:], picked(0)).then_inc(picked_b1, 1)
                    V.tensor_scalar(slot_id[:], slot_id[:], float(SLOTS), None, ALU.add).then_inc(slot_step, 1)
                    dve.wait_ge(slot_step, r)
                build(0, n0)
                if isinstance(r, int):
                    then(V.reduce_max(most[:], psum[:, 7, NTILE * E:(NTILE + 1) * E], AX.X))
                    V.tensor_copy(most_i[:], most[:]).then_inc(counts_ready, 1)
                with nc.vector.Fori(0, PAIRS - 1) as pair:
                    pair_steps(pair, reg(nc.vector, r * PAIRS + pair, ROUNDS * PAIRS), False)
                pair_steps(PAIRS - 1, reg(nc.vector, r * PAIRS + PAIRS - 1, ROUNDS * PAIRS), True)

            round_of(0)
            dve.wait_ge(counts_ready, 1)
            rounds_after_first(nc.vector, tokens_most(nc.vector), round_of)
            V.memset(most[:], 0.0).then_inc(moe_done, 1)
            dve.wait_ge(moe_done, 1)
            squares_of(2)

            dve.wait_ge(rms_ready, 3)
            dve.wait_ge(squares, NORM_SQUARES[2])
            dve.wait_ge(g_final_landed, 16)
            V.scalar_tensor_tensor(out=x_norm[:, 0, :], in0=x_acc[:, 0, :], scalar=rms[:, 2, 0:1], in1=gain[:],
                                   op0=ALU.mult, op1=ALU.mult).then_inc(final_ready[0], 1)
            dve.wait_ge(final_scaled, 2)
            V.tensor_tensor(x_norm[:, 1, :], x_norm[:, 1, :], gain[:], ALU.mult).then_inc(final_ready[1], 1)

        @block.gpsimd
        def _(pool):
            G = nc.gpsimd
            G.memset(ident[:], 0.0)
            G.memset(ones[:], 1.0).then_inc(pool_step, 1)
            pool.wait_ge(pool_step, 1)
            G.affine_select(out=ident[:], in_=ident[:], compare_op=ALU.not_equal, fill=1.0, base=0,
                            pattern=[[-1, P]], channel_multiplier=1).then_inc(consts_made, 1)
            G.affine_select(out=before[:], in_=ones[:], compare_op=ALU.is_ge, fill=0.0, base=-1,
                            pattern=[[1, P]], channel_multiplier=-1)
            G.iota(slot_id[:], pattern=[[1, SLOTS]], base=1, channel_multiplier=0, allow_small_or_imprecise_dtypes=True)
            G.iota(expert_id[:], pattern=[[1, E]], base=0, channel_multiplier=0, allow_small_or_imprecise_dtypes=True)
            G.iota(ramp[:], pattern=[[1, 16]], base=1, channel_multiplier=0,
                   allow_small_or_imprecise_dtypes=True).then_inc(consts_made, 1)
            pool.wait_ge(presets_made, 1)
            step = Counter(pool_step)
            step.n = 1
            for i in range(3):
                if i == 2:
                    pool.wait_ge(moe_done, 1)
                pool.wait_ge(squares, NORM_SQUARES[i])
                if i == 1:
                    step.inc(G.tensor_tensor(sumsq[:, i, :], sumsq[:, i, :], sumsq_right[:], ALU.add))
                    pool.wait_ge(pool_step, step.now())
                step.inc(G.tensor_scalar(rms[:, i, :], sumsq[:, i, :], 1.0 / D, EPS, ALU.mult, ALU.add))
                pool.wait_ge(pool_step, step.now())
                G.tensor_tensor(rms[:, i, :], rms[:, i, :], half[:], ALU.pow).then_inc(rms_ready, 1)
                if i == 0:
                    for c in range(4 * KD):
                        pool.wait_ge(w_high_ready, c + 1)
                        G.tensor_tensor(w_low[:, c // KD, c % KD, :], w_in_sb[:, c // KD, c % KD, :],
                                        w_high[:, c % 3, :].bitcast(F32), ALU.subtract).then_inc(w_low_ready, 1)
                    for c, (k, n) in enumerate(OUT_BLOCKS, IN_BLOCKS):
                        cols = slice(n * BANK, (n + 1) * BANK)
                        pool.wait_ge(w_high_ready, c + 1)
                        G.tensor_tensor(w_out_low[:, k, cols], w_out_sb[:, k, cols], w_high[:, c % 3, :].bitcast(F32),
                                        ALU.subtract).then_inc(w_low_ready, 1)
                elif i == 1:
                    pool.wait_ge(consts_landed, 16 * 10)
                    for t in (1, 2):
                        pool.wait_ge(scaled, NTILE + t)
                        G.tensor_tensor(x_norm[0:rows[t], t, :], x_norm[0:rows[t], t, :], gain[0:rows[t], :],
                                        ALU.mult).then_inc(x_norm_ready, 1)
            pool.wait_ge(g_final_landed, 16)
            pool.wait_ge(final_scaled, 1)
            G.tensor_tensor(x_norm[0:NS, 2, :], x_norm[0:NS, 2, :], gain[0:NS, :], ALU.mult).then_inc(final_ready[2], 1)


INPUTS = ["x_prompt", "x_sample", "state_conv", "state_pool", "norm_mix_g", "w_in", "conv_w", "pool_w",
          "pool_scale", "w_out", "norm_ffn_g", "router_w", "router_b", "exp_w1", "exp_b1", "exp_w2",
          "exp_b2", "final_norm_g"]


def kernel(**inputs):
    import numpy as np
    import concourse.bacc as bacc
    from concourse.bass_utils import run_bass_kernel_spmd

    nc = bacc.Bacc("TRN2", target_bir_lowering=False, num_devices=1)
    arrays, aps = {}, []
    for name in INPUTS:
        a = np.ascontiguousarray(inputs[name])
        arrays[f"in_{name}"] = a
        aps.append(nc.dram_tensor(f"in_{name}", a.shape, mybir.dt.from_np(a.dtype), kind="ExternalInput").ap())
    xp, xs, sc, sp = (inputs[n].shape for n in ("x_prompt", "x_sample", "state_conv", "state_pool"))
    shapes = [xp, xs, (sc[0], xp[0]) + tuple(sc[2:]), (sp[0], xp[0]) + tuple(sp[2:]), sc, sp]
    for i, shape in enumerate(shapes):
        aps.append(nc.dram_tensor(f"out_{i}", tuple(shape), F32, kind="ExternalOutput").ap())
    hybrid_moe_layer(nc, *aps)
    results = run_bass_kernel_spmd(nc, [arrays], core_ids=[0]).results[0]
    return tuple(results[f"out_{i}"] for i in range(len(shapes)))
```
